# Optimizing a Trainium2 kernel written in Bass

```python
import jax, jax.numpy as jnp
from jax import lax
import numpy as np

D_MODEL = 1024
BATCH = 1
SEQ = 1024
DEPTH = 1

CHUNK = 64
EPS = 1e-6
A_WIDTH = 512
CONV_WIDTH_A = 3
N_HEADS = 8
N_KV_HEADS = 2
HEAD_DIM = 64
WINDOW = 128
WINDOW_CHUNKS = WINDOW // CHUNK
SGU_LEN = 128
SGU_GROUPS = 4
SGU_WIDTH = 512
SGU_GROUP_DIM = SGU_WIDTH // SGU_GROUPS
N_BRANCH = 3
BRANCH_WIDTH = 512
D_FF = 2816
CONV_WIDTH_F = 3

SPLIT_SIZES = (A_WIDTH, A_WIDTH, A_WIDTH,
               N_HEADS * HEAD_DIM, N_KV_HEADS * HEAD_DIM, N_KV_HEADS * HEAD_DIM,
               SGU_WIDTH, SGU_WIDTH,
               N_BRANCH * D_MODEL)
D_IN = sum(SPLIT_SIZES)
SPLIT_POINTS = [int(c) for c in np.cumsum(SPLIT_SIZES)[:-1]]

kernel_name = 'hybrid_gated_conv_swa_sgu_convffn'

def rmsnorm(x, g):
    xf = x.astype(jnp.float32)
    y = xf * lax.rsqrt(jnp.mean(xf * xf, axis=-1, keepdims=True) + EPS)
    return (y * g).astype(x.dtype)

def causal_dwconv(x, w):
    K = w.shape[0]
    S = x.shape[1]
    xp = jnp.pad(x, ((0, 0), (K - 1, 0), (0, 0)))
    out = xp[:, 0:S] * w[0]
    for j in range(1, K):
        out = out + xp[:, j:j + S] * w[j]
    return out

def alibi_slopes(n):
    return jnp.asarray([2.0 ** (-8.0 * (i + 1) / n) for i in range(n)], dtype=jnp.float32)

def sliding_window_attention(q, k, v, q_gain, k_gain, sink):
    B, S, _ = q.shape
    n_chunks = S // CHUNK
    G = N_HEADS // N_KV_HEADS
    band = WINDOW_CHUNKS * CHUNK
    q = rmsnorm(q.reshape(B, S, N_HEADS, HEAD_DIM), q_gain).astype(jnp.float32)
    k = rmsnorm(k.reshape(B, S, N_KV_HEADS, HEAD_DIM), k_gain).astype(jnp.float32)
    v = v.reshape(B, S, N_KV_HEADS, HEAD_DIM)
    qc = q.reshape(B, n_chunks, CHUNK, N_KV_HEADS, G, HEAD_DIM)

    def banded(t):
        tc = t.reshape(B, n_chunks, CHUNK, N_KV_HEADS, HEAD_DIM)
        tp = jnp.pad(tc, ((0, 0), (WINDOW_CHUNKS - 1, 0), (0, 0), (0, 0), (0, 0)))
        return jnp.concatenate([tp[:, j:j + n_chunks] for j in range(WINDOW_CHUNKS)], axis=2)

    kb = banded(k)
    vb = banded(v)
    s = jnp.einsum('bnqkgd,bnskd->bnkgqs', qc, kb) * (HEAD_DIM ** -0.5)
    q_pos = (WINDOW_CHUNKS - 1) * CHUNK + jnp.arange(CHUNK)
    k_pos = jnp.arange(band)
    dist = jnp.abs(q_pos[:, None] - k_pos[None, :]).astype(jnp.float32)
    slopes = alibi_slopes(N_HEADS).reshape(N_KV_HEADS, G)
    s = s - slopes[:, :, None, None] * dist
    key_chunk = jnp.arange(n_chunks)[:, None] - (WINDOW_CHUNKS - 1) + k_pos[None, :] // CHUNK
    valid = key_chunk >= 0
    s = jnp.where(valid[None, :, None, None, None, :], s, -1e30)
    sink_l = sink.astype(jnp.float32).reshape(N_KV_HEADS, G)[None, None, :, :, None, None]
    m = jnp.maximum(jnp.max(s, axis=-1, keepdims=True), sink_l)
    e = jnp.exp(s - m)
    p = e / (jnp.sum(e, axis=-1, keepdims=True) + jnp.exp(sink_l - m))
    o = jnp.einsum('bnkgqs,bnskd->bnqkgd', p.astype(v.dtype), vb)
    return o.reshape(B, S, N_HEADS * HEAD_DIM)

def spatial_gating(u, v, norm_gain, w_s, b_s):
    B, S, _ = u.shape
    n = S // SGU_LEN
    v = rmsnorm(v, norm_gain).reshape(B, n, SGU_LEN, SGU_GROUPS, SGU_GROUP_DIM)
    t = jnp.arange(SGU_LEN)
    mask = (t[None, :] // CHUNK) <= (t[:, None] // CHUNK)
    w = jnp.where(mask[None], w_s, 0)
    mixed = jnp.einsum('gts,bnsgc->bntgc', w, v) + jnp.transpose(b_s)[:, :, None]
    return u * mixed.reshape(B, S, SGU_WIDTH)

def hybrid_layer(x, mix_norm_g, w_in, b_in, conv_a_w, q_norm_g, k_norm_g, attn_sink,
                 sgu_norm_g, sgu_w, sgu_b, w_branch, w_out, ffn_norm_g, w_up, conv_f_w, w_down):
    B, S, _ = x.shape
    h = rmsnorm(x, mix_norm_g)
    z = h @ w_in + b_in
    a_b, a_c, a_h, q, k, v, s_u, s_v, gate = jnp.split(z, SPLIT_POINTS, axis=-1)
    y_a = a_b * causal_dwconv(a_c * a_h, conv_a_w)
    y_b = sliding_window_attention(q, k, v, q_norm_g, k_norm_g, attn_sink)
    y_c = spatial_gating(jax.nn.gelu(s_u), jax.nn.gelu(s_v), sgu_norm_g, sgu_w, sgu_b)
    branches = jnp.stack([y_a, y_b, y_c], axis=2)
    proj = jnp.einsum('bsnc,ncd->bsnd', branches, w_branch)
    gates = jax.nn.sigmoid(gate.reshape(B, S, N_BRANCH, D_MODEL))
    merged = jnp.sum(gates * proj, axis=2)
    x = x + merged @ w_out
    hf = rmsnorm(x, ffn_norm_g)
    up = causal_dwconv(hf @ w_up, conv_f_w)
    g, val = jnp.split(up, 2, axis=-1)
    return x + (jax.nn.silu(g) * val) @ w_down

def setup_inputs(seed: int = 0) -> dict:
    key = jax.random.key(seed)
    ks = jax.random.split(key, 17)
    f32 = jnp.float32
    nrm = lambda k, shape, scale: jax.random.normal(k, shape, f32) * scale
    return {
        'x': nrm(ks[0], (BATCH, SEQ, D_MODEL), 1.0),
        'mix_norm_g': 1.0 + nrm(ks[1], (DEPTH, D_MODEL), 0.02),
        'w_in': nrm(ks[2], (DEPTH, D_MODEL, D_IN), D_MODEL ** -0.5),
        'b_in': nrm(ks[3], (DEPTH, D_IN), 0.02),
        'conv_a_w': nrm(ks[4], (DEPTH, CONV_WIDTH_A, A_WIDTH), CONV_WIDTH_A ** -0.5),
        'q_norm_g': 1.0 + nrm(ks[5], (DEPTH, HEAD_DIM), 0.02),
        'k_norm_g': 1.0 + nrm(ks[6], (DEPTH, HEAD_DIM), 0.02),
        'attn_sink': nrm(ks[7], (DEPTH, N_HEADS), 0.5),
        'sgu_norm_g': 1.0 + nrm(ks[8], (DEPTH, SGU_WIDTH), 0.02),
        'sgu_w': nrm(ks[9], (DEPTH, SGU_GROUPS, SGU_LEN, SGU_LEN), SGU_LEN ** -0.5),
        'sgu_b': 1.0 + nrm(ks[10], (DEPTH, SGU_GROUPS, SGU_LEN), 0.02),
        'w_branch': nrm(ks[11], (DEPTH, N_BRANCH, BRANCH_WIDTH, D_MODEL), BRANCH_WIDTH ** -0.5),
        'w_out': nrm(ks[12], (DEPTH, D_MODEL, D_MODEL), D_MODEL ** -0.5),
        'ffn_norm_g': 1.0 + nrm(ks[13], (DEPTH, D_MODEL), 0.02),
        'w_up': nrm(ks[14], (DEPTH, D_MODEL, 2 * D_FF), D_MODEL ** -0.5),
        'conv_f_w': nrm(ks[15], (DEPTH, CONV_WIDTH_F, 2 * D_FF), CONV_WIDTH_F ** -0.5),
        'w_down': nrm(ks[16], (DEPTH, D_FF, D_MODEL), D_FF ** -0.5),
    }

def reference(x, mix_norm_g, w_in, b_in, conv_a_w, q_norm_g, k_norm_g, attn_sink,
              sgu_norm_g, sgu_w, sgu_b, w_branch, w_out, ffn_norm_g, w_up, conv_f_w, w_down):
    for l in range(DEPTH):
        x = hybrid_layer(x, mix_norm_g[l], w_in[l], b_in[l], conv_a_w[l], q_norm_g[l],
                         k_norm_g[l], attn_sink[l], sgu_norm_g[l], sgu_w[l], sgu_b[l],
                         w_branch[l], w_out[l], ffn_norm_g[l], w_up[l], conv_f_w[l], w_down[l])
    return x


_drawn_inputs = setup_inputs


def setup_inputs(seed=0):
    import zlib

    import numpy as np

    out = dict(_drawn_inputs(seed))
    spreads = {}
    factors = {'q_norm_g': 8.0,
     'k_norm_g': 8.0,
     'attn_sink': 8.0,
     'sgu_norm_g': 8.0,
     'sgu_b': 8.0,
     'ffn_norm_g': 4.257}
    for name, (base, spread) in spreads.items():
        noise = np.random.default_rng([zlib.crc32(name.encode()), seed]).standard_normal(out[name].shape)
        drawn = base * np.exp(spread * noise) if base else spread * noise
        out[name] = __import__('jax').numpy.asarray(drawn.astype(out[name].dtype))
    for name, factor in factors.items():
        out[name] = (out[name] * factor).astype(out[name].dtype)
    return out
```

```python
from contextlib import ExitStack

import concourse.bass as bass
from concourse import mybir

F32 = mybir.dt.float32
F32R = mybir.dt.float32r
ALU = mybir.AluOpType
ACT = mybir.ActivationFunctionType
AX_X = mybir.AxisListType.X

P = 128
S = 1024
D = 1024
KD = D // P
NT = S // P
HALF = 512
BR = 512
KB = BR // P
HD = 64
CHUNK = 64
SG = 4
FF_TILES = 22
FF_STEPS = FF_TILES // 2
EPS = 1e-6
SBUF_BYTES = 212800

B_SV, B_K, B_V, B_Q, B_U = 0, 4, 5, 6, 10
B_GC, B_A, B_GA, B_GB, B_OUT, B_FF = 14, 30, 42, 58, 74, 82
C_SV, C_K, C_V, C_Q, C_U, C_GC, C_A, C_GA, C_GB = 0, 4, 5, 6, 10, 14, 22, 34, 42
Z_K, Z_V, Z_Q, Z_U, Z_GC, Z_A, Z_GA, Z_GB, Z_FF = 0, 1, 2, 6, 10, 26, 38, 54, 70


class Count:

    def __init__(self):
        self.n, self.shift = 0, 0

    def up(self):
        self.n += 1
        return self.n + self.shift

    def enter(self, i, first, per):
        self.start, self.per, self.shift = self.n, per, (i - first) * per

    def leave(self, trips):
        assert self.n - self.start == self.per, (self.n - self.start, self.per)
        self.n, self.shift = self.start + self.per * trips, 0


def hybrid_layer(nc, x, w_in, bias, w_branch, w_out, w_up, w_down, mix_g, ffn_g, sv_bias, sgu_wt,
                 sgu_b, sgu_g, conv_a, conv_f, q_gain, k_gain, sink, alibi, ident, head_ones, out):
    with ExitStack() as ctx:
        base = nc.sbuf_base
        ctx.enter_context(nc.sbuf_tensor("arena", [P, SBUF_BYTES // 4], F32))

        def at(name, offset, shape, dt=F32):
            size = 4
            for n in shape[1:]:
                size *= n
            assert offset + size <= SBUF_BYTES - 32, (name, offset + size)
            start = (base + 31) // 32 * 32
            return nc.alloc_sbuf_tensor_at(name, shape, dt, offset=start + offset)

        K1 = 1024
        R1, MG, YB, QR = 0, 64 * K1, 96 * K1, 128 * K1
        RING = QR + 46336
        TMP = RING + 24 * K1
        CST = TMP + 8 * K1

        h_hi = at("h_hi", R1, [P, KD, S], F32R)
        h_lo = at("h_lo", R1 + 32 * K1, [P, KD, S], F32R)
        merged = at("merged", MG, [P, KD, S])
        x1 = at("x1", MG, [P, NT, D])
        vhat = at("vhat", MG, [P, NT, BR])
        x_in = at("x_in", MG + 16 * K1, [P, 4, D])
        raw_k = at("raw_k", MG + 16 * K1, [P, S])
        square = at("square", MG + 20 * K1, [P, S])
        mean = at("mean", MG + 24 * K1, [P, S])
        rstd = at("rstd", MG + 28 * K1, [P, S])
        y_hi = at("y_hi", YB, [P, KB, S], F32R)
        y_lo = at("y_lo", YB + 16 * K1, [P, KB, S], F32R)
        wide_y_hi = at("wide_y_hi", YB, [P, KD, HALF], F32R)
        wide_y_lo = at("wide_y_lo", YB + 16 * K1, [P, KD, HALF], F32R)
        q = at("q", QR, [P, 4, S])
        v_win = at("v_win", QR + 16384, [P, 16, P])
        k_pad = at("k_pad", QR + 24576, [P, CHUNK + S])
        alibi_sb = at("alibi_sb", QR + 28928, [P, 2, HALF])
        q_st = at("q_st", QR + 33024, [P, 2, 2, 4, CHUNK])
        v_st = at("v_st", QR + 37120, [P, 2, P])
        probs = at("probs", QR + 38144, [P, 2 * HALF])
        probs_t = at("probs_t", QR + 42240, [P, 2, HALF])
        v_pad = at("v_pad", QR + 28928, [P, CHUNK + S])
        mix_g_sb = at("mix_g_sb", QR + 38144, [P, D])
        newton = at("newton", QR + 38144, [P, S])
        row_sb = at("row_sb", QR + 42240, [P, BR])
        sgu_wt_sb = at("sgu_wt_sb", QR + 42240 + 2048, [P, SG, P])
        a_c = at("a_c", QR + 16384, [P, S])
        a_conv = at("a_conv", QR + 20480, [P, S])
        a_ch = at("a_ch", QR + 24576, [P, 2 + S])
        a_y = at("a_y", QR + 28928, [P, S])
        wide_q_hi = at("wide_q_hi", QR, [P, KD, HALF], F32R)
        wide_q_lo = at("wide_q_lo", QR + 16384, [P, KD, HALF], F32R)
        x_norm = at("x_norm", QR + 33024, [P, 2, D])
        ffn_g_sb = at("ffn_g_sb", QR + 41216, [P, D])
        wd_hi = at("wd_hi", QR, [P, 2, D], F32R)
        wd_lo = at("wd_lo", QR + 8192, [P, 2, D], F32R)
        up_g = at("up_g", QR + 16384, [P, 2 + S])
        up_v = at("up_v", QR + 20512, [P, 2 + S])
        conv_g = at("conv_g", QR + 24640, [P, S])
        conv_v = at("conv_v", QR + 28736, [P, S])
        raw = at("raw", RING, [P, 2, D])
        ring_hi = at("ring_hi", RING + 8 * K1, [P, 2, D], F32R)
        ring_lo = at("ring_lo", RING + 16 * K1, [P, 2, D], F32R)
        gate = at("gate", TMP, [P, S])
        prod = at("prod", TMP + 4 * K1, [P, S])
        place = [CST]

        def small(name, shape):
            t = at(name, place[0], shape)
            n = 4
            for m in shape[1:]:
                n *= m
            place[0] += (n + 31) // 32 * 32
            return t

        ident_sb = small("ident_sb", [P, P])
        ones_sb = small("ones_sb", [P, P])
        bias_sb = small("bias_sb", [P, 50])
        conv_f_sb = small("conv_f_sb", [P, 2 * FF_TILES * 3])
        conv_a_sb = small("conv_a_sb", [P, KB * 3])
        q_gain_sb = small("q_gain_sb", [P, 1])
        q_scale_sb = small("q_scale_sb", [P, 1])
        k_gain_sb = small("k_gain_sb", [P, 1])
        sgu_g_sb = small("sgu_g_sb", [P, SG])
        sink_sb = small("sink_sb", [P, 8])
        peak = small("peak", [P, 8])
        sink_e = small("sink_e", [P, 8])
        denom = small("denom", [P, 8])
        power = small("power", [P, 1])
        sumsq = small("sumsq", [P, 3 * NT])
        meansq = small("meansq", [P, 3 * NT])
        rs = small("rs", [P, 3 * NT])

        psum = ctx.enter_context(nc.psum_tensor("psum", [P, 8, HALF], F32))

        def pair(n):
            return psum[:, 2 * n:2 * n + 2, :].rearrange("p a b -> p (a b)")

        def sem(name):
            return ctx.enter_context(nc.semaphore(name))

        raw_in = [sem(f"raw_in{n}") for n in range(2)]
        xt_in = [sem(f"xt_in{n}") for n in range(4)]
        c_in = sem("c_in")
        alibi_in = sem("alibi_in")
        row_in = sem("row_in")
        ffn_g_in = sem("ffn_g_in")
        out_done = sem("out_done")
        w_hi = sem("w_hi")
        w_lo = sem("w_lo")
        z_done = sem("z_done")
        act_z = sem("act_z")
        dve_z = sem("dve_z")
        pair2_read = sem("pair2_read")
        pair3_read = sem("pair3_read")
        squared = sem("squared")
        rs_ready = sem("rs_ready")
        pool_step = sem("pool_step")
        zeroed = sem("zeroed")
        x_norm_ready = sem("x_norm_ready")
        turned = sem("turned")
        turned_hi = sem("turned_hi")
        turned_lo = sem("turned_lo")
        sv_done = sem("sv_done")
        sv_biased = sem("sv_biased")
        sv_gelu = sem("sv_gelu")
        vhat_ready = sem("vhat_ready")
        qk_sq = sem("qk_sq")
        qk_sum = sem("qk_sum")
        qk_root = sem("qk_root")
        qk_ready = sem("qk_ready")
        v_ready = sem("v_ready")
        v_turned = sem("v_turned")
        u_ready = sem("u_ready")
        mixed = sem("mixed")
        y_ready = sem("y_ready")
        y_hi_done = sem("y_hi_done")
        y_lo_done = sem("y_lo_done")
        staged = sem("staged")
        scores = sem("scores")
        shifted = sem("shifted")
        exps = sem("exps")
        probs_ready = sem("probs_ready")
        probs_turned = sem("probs_turned")
        probs_t_ready = sem("probs_t_ready")
        attended = sem("attended")
        ac_ready = sem("ac_ready")
        m_hi = sem("m_hi")
        m_lo = sem("m_lo")
        o_done = sem("o_done")
        x1_add = sem("x1_add")
        conv_done = sem("conv_done")
        silu_done = sem("silu_done")
        act_made = sem("act_made")
        d_done = sem("d_done")
        masked = sem("masked")
        merge_add = sem("merge_add")
        dve_step = sem("dve_step")

        block = ctx.enter_context(nc.Block())

        @block.sync
        def _(sp):
            def load(const, per, i, src, width=D):
                slot = const % 2
                if const >= 2:
                    sp.wait_ge(w_lo, const - 1 + per * i)
                sp.dma_start(raw[:, slot, 0:width], src).then_inc(raw_in[slot], 16)

            def load_x(t):
                sp.dma_start(x_in[:, t % 4, :], x[t * P:(t + 1) * P, :]).then_inc(xt_in[t % 4], 16)

            load_x(0)
            sp.dma_start(ident_sb[:, :], ident).then_inc(c_in, 16)
            sp.dma_start(mix_g_sb[:, :], mix_g.to_broadcast([P, D])).then_inc(c_in, 16)
            load(B_SV, 0, 0, w_in[C_SV])
            load_x(1)
            load(B_SV + 1, 0, 0, w_in[C_SV + 1])
            sp.dma_start(row_sb[:, :], sv_bias.to_broadcast([P, BR])).then_inc(row_in, 16)
            for dst, src in ((ones_sb, head_ones), (bias_sb, bias), (conv_f_sb, conv_f), (conv_a_sb, conv_a),
                             (q_gain_sb, q_gain), (k_gain_sb, k_gain), (sgu_g_sb, sgu_g),
                             (sgu_wt_sb, sgu_wt)):
                full = dst[:, :, :].rearrange("p a b -> p (a b)") if dst is sgu_wt_sb else dst[:, :]
                sp.dma_start(full, src).then_inc(c_in, 16)
            for b in range(2):
                sp.dma_start(sink_sb[b * HD:(b + 1) * HD, 0:4], sink[b:b + 1, :].to_broadcast([HD, 4])).then_inc(c_in, 16)
            load_x(2)
            load_x(3)
            load(B_SV + 2, 0, 0, w_in[C_SV + 2])
            load(B_SV + 3, 0, 0, w_in[C_SV + 3])
            for t in range(4, NT):
                sp.wait_ge(turned, t - 3)
                load_x(t)
            for c in range(4, 6):
                load(c, 0, 0, w_in[c])
            sp.wait_ge(sv_biased, NT)
            sp.dma_start(row_sb[:, :], sgu_b.to_broadcast([P, BR])).then_inc(row_in, 16)
            for c in range(6, 10):
                load(c, 0, 0, w_in[c])
            sp.wait_ge(pair3_read, 2)
            sp.dma_start(alibi_sb[:, :, :].rearrange("p a b -> p (a b)"), alibi).then_inc(alibi_in, 16)
            for c in range(10, 14):
                load(c, 0, 0, w_in[c])

            def gate_loads(b0, c0, n):
                with sp.Fori(0, KD) as i:
                    load(b0, 2, i, w_in[c0 + i])
                    load(b0 + 1, 2, i, w_branch[n * KD + i], KB * P)

            gate_loads(B_GC, C_GC, 0)
            with sp.Fori(0, 2) as i:
                for c in range(6):
                    load(B_A + c, 6, i, w_in[C_A + c + 6 * i])
            gate_loads(B_GA, C_GA, 1)
            gate_loads(B_GB, C_GB, 2)
            for c in range(2 * KB):
                load(B_OUT + c, 0, 0, w_out[c])
            sp.wait_ge(m_lo, NT)
            for n in range(4):
                sp.dma_start(x1[:, 2 * n:2 * n + 2, :], x[2 * n * P:(2 * n + 2) * P, :].rearrange("(t p) d -> p t d", p=P)).then_inc(xt_in[n], 16)
            sp.dma_start(ffn_g_sb[:, :], ffn_g.to_broadcast([P, D])).then_inc(ffn_g_in, 16)
            with sp.Fori(0, FF_STEPS) as i:
                load(B_FF, 6, i, w_up[4 * i])
                load(B_FF + 1, 6, i, w_up[4 * i + 1])
                load(B_FF + 2, 6, i, w_up[4 * i + 2])
                load(B_FF + 3, 6, i, w_down[2 * i])
                load(B_FF + 4, 6, i, w_down[2 * i + 1])
                load(B_FF + 5, 6, i, w_up[4 * i + 3])
            for t in range(NT):
                sp.wait_ge(x1_add, 2 * NT + NT * (FF_STEPS - 1) + t + 1)
                sp.dma_start(out[t * P:(t + 1) * P, :], x1[:, t, :]).then_inc(out_done, 16)
            sp.wait_ge(out_done, 16 * NT)

        @block.gpsimd
        def _(pool):
            n = Count()
            pool.memset(power[:, :], -0.5).then_inc(pool_step, 1)
            pool.wait_ge(pool_step, n.up())
            pool.wait_ge(c_in, 16 * 12)
            pool.memset(sgu_wt_sb[CHUNK:P, :, 0:CHUNK], 0.0).then_inc(masked, 1)
            pool.wait_ge(masked, 1)

            def row_rs(col, need, width):
                pool.wait_ge(squared, need)
                pool.tensor_scalar(meansq[:, col:col + 1], sumsq[:, col:col + 1], 1.0 / width, EPS,
                                   ALU.mult, ALU.add).then_inc(pool_step, 1)
                pool.wait_ge(pool_step, n.up())
                pool.tensor_tensor(rs[:, col:col + 1], meansq[:, col:col + 1], power[:, :],
                                   ALU.pow).then_inc(rs_ready, 1)

            order = 0
            for step in range(NT + 2):
                for lag, col, width in ((0, 0, D), (2, NT, BR)):
                    t = step - lag
                    if 0 <= t < NT:
                        order += 1
                        row_rs(col + t, order, width)
            pool.memset(v_pad[:, 0:CHUNK], 0.0).then_inc(zeroed, 1)
            pool.memset(k_pad[:, 0:CHUNK], 0.0).then_inc(zeroed, 1)
            pool.wait_ge(pair3_read, 2)
            for g in range(2):
                rows = slice((1 - g) * HD, (2 - g) * HD)
                pool.memset(q_st[rows, g, :, :, :].rearrange("p c j t -> p (c j t)"), 0.0).then_inc(pool_step, 1)
                pool.wait_ge(pool_step, n.up())
            pool.wait_ge(qk_ready, 5)

            def stage(i):
                for g in range(2):
                    rows = slice(g * HD, (g + 1) * HD)
                    pool.tensor_copy(q_st[rows, g, :, :, :], q[rows, :, bass.ds(i * P, P)].rearrange("p j (c t) -> p c j t", t=CHUNK)).then_inc(staged, 1)
                    pool.wait_ge(staged, 3 * i + g + 1)
                pool.tensor_copy(v_st[:, :, :], v_win[:, bass.ds(2 * i, 2), :]).then_inc(staged, 1)

            stage(0)
            with pool.Fori(1, NT) as i:
                pool.wait_ge(attended, i)
                stage(i)
            pool.wait_ge(attended, NT)
            pool.memset(a_ch[:, 0:2], 0.0).then_inc(zeroed, 1)
            for t in range(NT):
                row_rs(2 * NT + t, 2 * NT + t + 1, D)
            pool.wait_ge(o_done, NT)
            pool.memset(up_g[:, 0:2], 0.0).then_inc(zeroed, 1)
            pool.memset(up_v[:, 0:2], 0.0).then_inc(zeroed, 1)

        @block.scalar
        def _(act):
            def hi(const, per, i, dst, tiles=KD):
                slot = const % 2
                act.wait_ge(raw_in[slot], 16 * (const // 2 + 1) + 8 * per * i)
                src = raw[:, slot, 0:tiles * P]
                if len(dst.shape) == 3:
                    src = src.rearrange("p (k n) -> p k n", n=dst.shape[2])
                act.activation(dst, src, ACT.Copy).then_inc(w_hi, 1)

            def ring_hi_of(const, per, i, z, per_z, tiles=KD):
                if z >= 2:
                    act.wait_ge(z_done, z - 1 + per_z * i)
                hi(const, per, i, ring_hi[:, z % 2, 0:tiles * P], tiles)

            def rows_squared(src, col):
                act.activation(gate[:, 0:src.shape[1]], src, ACT.Square,
                               accum_out=sumsq[:, col:col + 1]).then_inc(squared, 1)

            n_squared = 0
            for step in range(NT + 2):
                if step < NT:
                    act.wait_ge(xt_in[step % 4], 16 * (step // 4 + 1))
                    if n_squared:
                        act.wait_ge(squared, n_squared)
                    rows_squared(x_in[:, step % 4, :], step)
                    n_squared += 1
                if step < 2:
                    for b in (2 * step, 2 * step + 1):
                        hi(b, 0, 0, wide_y_hi[:, :, b * P:(b + 1) * P])
                if step in (4, 5):
                    ring_hi_of(step, 0, 0, step - 4, 0)
                t = step - 1
                if 0 <= t < NT:
                    act.wait_ge(turned, t + 1)
                    act.activation(h_hi[:, :, t * P:(t + 1) * P],
                                   pair(t % 2).rearrange("p (k n) -> p k n", n=P), ACT.Copy).then_inc(turned_hi, 1)
                t = step - 2
                if 0 <= t < NT:
                    act.wait_ge(sv_biased, t + 1)
                    act.activation(vhat[:, t, :], vhat[:, t, :], ACT.Gelu_apprx_tanh).then_inc(sv_gelu, 1)
                    act.wait_ge(sv_gelu, t + 1)
                    act.wait_ge(squared, n_squared)
                    rows_squared(vhat[:, t, :], NT + t)
                    n_squared += 1

            def evac(z, dst, func=ACT.Identity, col=0):
                act.wait_ge(z_done, z + 1)
                return act.activation(dst, pair(z % 2), func, bias=bias_sb[:, col:col + 1])

            def qk_square(n):
                if n:
                    act.wait_ge(qk_sum, n)
                act.activation(square[:, :], raw_k[:, :] if n == 0 else q[:, n - 1, :], ACT.Square).then_inc(qk_sq, 1)

            def qk_sqrt(n):
                act.wait_ge(pair2_read, n + 1)
                if n:
                    act.wait_ge(qk_ready, n)
                act.activation(rstd[:, :], mean[:, :], ACT.Sqrt).then_inc(qk_root, 1)

            act.wait_ge(c_in, 16 * 12)
            act.wait_ge(squared, 2 * NT)
            evac(Z_K, raw_k[:, :], col=C_K).then_inc(act_z, 1)
            ring_hi_of(B_Q, 0, 0, Z_Q, 0)
            act.wait_ge(act_z, 1)
            qk_square(0)
            evac(Z_V, v_pad[:, CHUNK:], col=C_V).then_inc(act_z, 1)
            ring_hi_of(B_Q + 1, 0, 0, Z_Q + 1, 0)
            for n in range(4):
                evac(Z_Q + n, q[:, n, :], col=C_Q + n).then_inc(act_z, 1)
                ring_hi_of(B_Q + n + 2, 0, 0, Z_Q + n + 2, 0)
                act.wait_ge(act_z, 3 + n)
                qk_square(n + 1)
                qk_sqrt(n)
            for n in range(SG):
                if n:
                    act.wait_ge(y_ready, n)
                if n == SG - 1:
                    ring_hi_of(B_GC, 0, 0, Z_GC, 0)
                evac(Z_U + n, gate[:, :], ACT.Gelu_apprx_tanh, C_U + n).then_inc(act_z, 1)
                if n < 2:
                    ring_hi_of(B_U + n + 2, 0, 0, Z_U + n + 2, 0)
                if n == 0:
                    qk_sqrt(4)
                act.wait_ge(y_ready, n + 1)
                act.activation(y_hi[:, n, :], prod[:, :], ACT.Copy).then_inc(y_hi_done, 1)

            def gates(b0, z0, c0, dve0, after, attention=False):
                def step(i, last):
                    ring_hi_of(b0 + 1, 2, i, z0 + 1, 2, KB)
                    if attention:
                        act.wait_ge(shifted, 2 * i + 2)
                        act.activation(probs[:, :], probs[:, :], ACT.Exp).then_inc(exps, 1)
                        act.activation(sink_e[:, :], sink_e[:, :], ACT.Exp).then_inc(exps, 1)
                    act.wait_ge(z_done, z0 + 1 + 2 * i)
                    act.wait_ge(dve_z, dve0 + i)
                    act.activation(gate[:, :], pair(0), ACT.Sigmoid, bias=bias_sb[:, bass.ds(c0 + i, 1)]).then_inc(act_z, 1)
                    if attention:
                        act.wait_ge(probs_turned, i + 1)
                        act.activation(probs_t[:, :, :].rearrange("p a b -> p (a b)"), pair(3), ACT.Copy).then_inc(probs_t_ready, 1)
                    if last:
                        after()
                    else:
                        ring_hi_of(b0 + 2, 2, i, z0 + 2, 2)

                with act.Fori(0, KD - 1) as i:
                    step(i, False)
                step(KD - 1, True)

            gates(B_GC, Z_GC, C_GC, 8, lambda: ring_hi_of(B_A, 0, 0, Z_A, 0), attention=True)

            act.wait_ge(pair3_read, 2 + SG + NT)
            for j in range(KB):
                z, b = Z_A + 3 * j, B_A + 3 * j
                ring_hi_of(b + 1, 0, 0, z + 1, 0)
                act.wait_ge(z_done, z + 1)
                act.wait_ge(dve_z, 15 + 2 * j)
                act.activation(a_c[:, :], pair(z % 2), ACT.Identity, bias=bias_sb[:, C_A + 3 * j:C_A + 3 * j + 1]).then_inc(act_z, 1)
                ring_hi_of(b + 2, 0, 0, z + 2, 0)
                ring_hi_of(b + 3, 0, 0, z + 3, 0)
                act.wait_ge(dve_z, 18 + 2 * j)
                act.activation(y_hi[:, j, :], a_y[:, :], ACT.Copy).then_inc(y_hi_done, 1)
            gates(B_GA, Z_GA, C_GA, 24, lambda: ring_hi_of(B_GB, 0, 0, Z_GB, 0))
            act.wait_ge(z_done, Z_GB)
            for n in range(KB):
                act.activation(y_hi[:, n, :], q[:, n, :], ACT.Copy).then_inc(y_hi_done, 1)

            def out_hi():
                act.wait_ge(y_lo_done, 3 * KB)
                for c in range(4):
                    hi(B_OUT + c, 0, 0, wide_q_hi[:, :, c * P:(c + 1) * P])

            gates(B_GB, Z_GB, C_GB, 32, out_hi)
            act.wait_ge(merge_add, 2 * KD)
            for t in range(NT):
                act.activation(h_hi[:, :, t * P:(t + 1) * P], merged[:, :, t * P:(t + 1) * P], ACT.Copy).then_inc(m_hi, 1)
            act.wait_ge(z_done, Z_FF)
            for c in range(4):
                hi(B_OUT + 4 + c, 0, 0, wide_y_hi[:, :, c * P:(c + 1) * P])
            for t in range(NT):
                act.wait_ge(x1_add, NT + t + 1)
                act.wait_ge(squared, 2 * NT + t)
                rows_squared(x1[:, t, :], 2 * NT + t)
                if t in (2, 3):
                    ring_hi_of(B_FF + t - 2, 0, 0, Z_FF + t - 2, 0)
                if t:
                    act.wait_ge(turned, NT + t)
                    act.activation(h_hi[:, :, (t - 1) * P:t * P],
                                   pair(2 + (t - 1) % 2).rearrange("p (k n) -> p k n", n=P), ACT.Copy).then_inc(turned_hi, 1)
            act.wait_ge(turned, 2 * NT)
            act.activation(h_hi[:, :, (NT - 1) * P:], pair(3).rearrange("p (k n) -> p k n", n=P), ACT.Copy).then_inc(turned_hi, 1)
            act.wait_ge(zeroed, 5)

            def up_evac(z, i, dst):
                act.wait_ge(z_done, z + 1 + 4 * i)
                act.activation(dst[:, 2:], pair(z % 2), ACT.Copy).then_inc(act_z, 1)

            def silu(n, i):
                act.wait_ge(conv_done, n + 4 * i)
                act.activation(conv_g[:, :], conv_g[:, :], ACT.Silu).then_inc(silu_done, 1)

            def last_val(i):
                act.wait_ge(conv_done, 4 * i - 2)
                up_evac(Z_FF - 1, i, up_v)
                act.wait_ge(act_made, 2 * i)
                act.activation(y_hi[:, 1, :], conv_v[:, :], ACT.Copy).then_inc(y_hi_done, 1)

            def ffn(i, first):
                if not first:
                    ring_hi_of(B_FF, 6, i, Z_FF, 4)
                    last_val(i)
                    ring_hi_of(B_FF + 1, 6, i, Z_FF + 1, 4)
                    act.wait_ge(conv_done, 4 * i - 1)
                up_evac(Z_FF, i, up_g)
                ring_hi_of(B_FF + 2, 6, i, Z_FF + 2, 4)
                silu(1, i)
                if first:
                    act.wait_ge(o_done, NT)
                else:
                    act.wait_ge(d_done, NT * i)
                for c in range(2):
                    hi(B_FF + 3 + c, 6, i, wd_hi[:, c, :])
                if not first:
                    act.wait_ge(conv_done, 4 * i)
                up_evac(Z_FF + 1, i, up_v)
                ring_hi_of(B_FF + 5, 6, i, Z_FF + 3, 4)
                act.wait_ge(act_made, 2 * i + 1)
                act.activation(y_hi[:, 0, :], conv_v[:, :], ACT.Copy).then_inc(y_hi_done, 1)
                act.wait_ge(conv_done, 4 * i + 1)
                up_evac(Z_FF + 2, i, up_g)
                silu(3, i)

            ffn(0, True)
            with act.Fori(1, FF_STEPS) as i:
                ffn(i, False)
            last_val(FF_STEPS)

        @block.vector
        def _(dve):
            n = Count()

            def lo(const, per, i, dst, part, tiles=KD):
                slot = const % 2
                src = raw[:, slot, 0:tiles * P]
                if len(dst.shape) == 3:
                    src = src.rearrange("p (k n) -> p k n", n=dst.shape[2])
                dve.wait_ge(w_hi, const + 1 + per * i)
                dve.tensor_tensor(dst, src, part.bitcast(F32), ALU.subtract).then_inc(w_lo, 1)

            def ring_lo_of(const, per, i, z, tiles=KD):
                w = tiles * P
                lo(const, per, i, ring_lo[:, z % 2, 0:w], ring_hi[:, z % 2, 0:w], tiles)

            dve.wait_ge(c_in, 16 * 12)
            dve.wait_ge(row_in, 16)
            dve.tensor_copy(sink_sb[:, 4:8], sink_sb[:, 0:4]).then_inc(dve_step, 1)
            dve.tensor_scalar(q_scale_sb[:, :], q_gain_sb[:, :], HD ** -0.5, None, ALU.mult).then_inc(dve_step, 1)
            n.up()
            dve.wait_ge(dve_step, n.up())
            seen, x_rs, v_rs = 0, {}, {}
            for step in range(NT + 2):
                for lag, where in ((0, x_rs), (2, v_rs)):
                    if 0 <= step - lag < NT:
                        seen += 1
                        where[step - lag] = seen
            for step in range(NT + 3):
                if step < NT:
                    t = step
                    dve.wait_ge(rs_ready, x_rs[t])
                    dve.scalar_tensor_tensor(out=x_in[:, t % 4, :], in0=x_in[:, t % 4, :], scalar=rs[:, t:t + 1],
                                             in1=mix_g_sb[:, :], op0=ALU.mult, op1=ALU.mult).then_inc(x_norm_ready, 1)
                if step < 2:
                    for b in (2 * step, 2 * step + 1):
                        cols = slice(b * P, (b + 1) * P)
                        lo(b, 0, 0, wide_y_lo[:, :, cols], wide_y_hi[:, :, cols])
                if step in (4, 5):
                    ring_lo_of(step, 0, 0, step - 4)
                t = step - 1
                if 0 <= t < NT:
                    dve.wait_ge(turned_hi, t + 1)
                    cols = slice(t * P, (t + 1) * P)
                    dve.tensor_tensor(h_lo[:, :, cols], pair(t % 2).rearrange("p (k n) -> p k n", n=P),
                                      h_hi[:, :, cols].bitcast(F32), ALU.subtract).then_inc(dve_z, 1)
                t = step - 2
                if 0 <= t < NT:
                    dve.wait_ge(sv_done, t + 1)
                    dve.tensor_tensor(vhat[:, t, :], psum[:, 4 + t % 2, :], row_sb[:, :], ALU.add).then_inc(sv_biased, 1)
                t = step - 3
                if 0 <= t < NT:
                    dve.wait_ge(rs_ready, v_rs[t])
                    dve.tensor_scalar(vhat[:, t, :], vhat[:, t, :], rs[:, NT + t:NT + t + 1], None,
                                      ALU.mult).then_inc(vhat_ready, 1)

            def qk_norm(m):
                raw_t = raw_k[:, :] if m == 0 else q[:, m - 1, :]
                dst = k_pad[:, CHUNK:] if m == 0 else q[:, m - 1, :]
                gain = k_gain_sb if m == 0 else q_scale_sb
                dve.wait_ge(qk_sum, m + 1)
                dve.tensor_scalar(mean[:, :], pair(2), 1.0 / HD, EPS, ALU.mult, ALU.add).then_inc(pair2_read, 1)
                dve.wait_ge(qk_root, m + 1)
                dve.reciprocal(rstd[:, :], rstd[:, :]).then_inc(dve_step, 1)
                dve.wait_ge(dve_step, n.up())
                dve.tensor_tensor(newton[:, :], rstd[:, :], rstd[:, :], ALU.mult).then_inc(dve_step, 1)
                dve.wait_ge(dve_step, n.up())
                dve.scalar_tensor_tensor(out=newton[:, :], in0=mean[:, :], scalar=-0.5, in1=newton[:, :],
                                         op0=ALU.mult, op1=ALU.mult).then_inc(dve_step, 1)
                dve.wait_ge(dve_step, n.up())
                dve.scalar_tensor_tensor(out=rstd[:, :], in0=newton[:, :], scalar=1.5, in1=rstd[:, :],
                                         op0=ALU.add, op1=ALU.mult).then_inc(dve_step, 1)
                dve.wait_ge(dve_step, n.up())
                dve.scalar_tensor_tensor(out=dst, in0=raw_t, scalar=gain[:, 0:1], in1=rstd[:, :],
                                         op0=ALU.mult, op1=ALU.mult).then_inc(qk_ready, 1)

            def windows(half):
                dve.wait_ge(v_turned, half + 1)
                dve.tensor_copy(v_win[:, 8 * half:8 * half + 8, :].rearrange("p a b -> p (a b)"), pair(3)).then_inc(pair3_read, 1)

            ring_lo_of(B_Q, 0, 0, Z_Q)
            ring_lo_of(B_Q + 1, 0, 0, Z_Q + 1)
            qk_norm(0)
            ring_lo_of(B_Q + 2, 0, 0, Z_Q + 2)
            windows(0)
            ring_lo_of(B_Q + 3, 0, 0, Z_Q + 3)
            qk_norm(1)
            windows(1)
            ring_lo_of(B_U, 0, 0, Z_U)
            qk_norm(2)
            ring_lo_of(B_U + 1, 0, 0, Z_U + 1)
            qk_norm(3)

            def split_y(row, src, k):
                dve.wait_ge(y_hi_done, k)
                dve.tensor_tensor(y_lo[:, row, :], src, y_hi[:, row, :].bitcast(F32), ALU.subtract).then_inc(y_lo_done, 1)
                dve.wait_ge(y_lo_done, k)

            dve.wait_ge(row_in, 32)
            for g in range(SG):
                if g < 2:
                    ring_lo_of(B_U + g + 2, 0, 0, Z_U + g + 2)
                if g == 0:
                    qk_norm(4)
                if g == SG - 1:
                    ring_lo_of(B_GC, 0, 0, Z_GC)
                dve.wait_ge(mixed, g + 1)
                dve.scalar_tensor_tensor(
                    out=prod[:, :].rearrange("p (a b) -> p a b", b=P), in0=pair(3).rearrange("p (a b) -> p a b", b=P),
                    scalar=sgu_g_sb[:, g:g + 1], in1=row_sb[:, g * P:(g + 1) * P].unsqueeze(1).to_broadcast([P, NT, P]),
                    op0=ALU.mult, op1=ALU.add).then_inc(pair3_read, 1)
                dve.wait_ge(pair3_read, 3 + g)
                dve.wait_ge(act_z, 7 + g)
                dve.tensor_tensor(prod[:, :], prod[:, :], gate[:, :], ALU.mult).then_inc(y_ready, 1)
                split_y(g, prod[:, :], g + 1)

            def merge(i, z0, act0, into):
                dve.wait_ge(z_done, z0 + 2 + 2 * i)
                dve.wait_ge(act_z, act0 + 1 + i)
                row = merged[:, bass.ds(i, 1), :].rearrange("p a b -> p (a b)")
                if not into:
                    dve.tensor_tensor(row, pair(1), gate[:, :], ALU.mult).then_inc(dve_z, 1)
                    return
                dve.tensor_tensor(prod[:, :], pair(1), gate[:, :], ALU.mult).then_inc(dve_z, 1)
                dve.wait_ge(dve_z, into + i)
                dve.tensor_tensor(row, row, prod[:, :], ALU.add).then_inc(merge_add, 1)
                dve.wait_ge(merge_add, into - 24 + i)

            def softmax_shift(i):
                tiles = probs[:, :].rearrange("p (a b) -> p a b", b=P)
                dve.wait_ge(scores, i + 1)
                dve.tensor_tensor(probs[:, :], pair(2), alibi_sb[:, :, :].rearrange("p a b -> p (a b)"), ALU.add).then_inc(pair2_read, 1)
                dve.wait_ge(pair2_read, 6 + i)
                dve.tensor_reduce(peak[:, :], tiles, AX_X, ALU.max).then_inc(dve_step, 1)
                dve.wait_ge(dve_step, n.up())
                dve.tensor_tensor(peak[:, :], peak[:, :], sink_sb[:, :], ALU.max).then_inc(dve_step, 1)
                dve.wait_ge(dve_step, n.up())
                dve.tensor_tensor(tiles, tiles, peak[:, :].unsqueeze(2).to_broadcast([P, 8, P]), ALU.subtract).then_inc(shifted, 1)
                dve.tensor_tensor(sink_e[:, :], sink_sb[:, :], peak[:, :], ALU.subtract).then_inc(shifted, 1)
                dve.tensor_copy(alibi_sb[:, 0, :], alibi_sb[:, 1, :]).then_inc(dve_step, 1)
                dve.wait_ge(dve_step, n.up())

            def softmax_scale(i):
                tiles = probs[:, :].rearrange("p (a b) -> p a b", b=P)
                dve.wait_ge(exps, 2 * i + 2)
                dve.tensor_reduce(denom[:, :], tiles, AX_X, ALU.add).then_inc(dve_step, 1)
                dve.wait_ge(dve_step, n.up())
                dve.tensor_tensor(denom[:, :], denom[:, :], sink_e[:, :], ALU.add).then_inc(dve_step, 1)
                dve.wait_ge(dve_step, n.up())
                dve.reciprocal(denom[:, :], denom[:, :]).then_inc(dve_step, 1)
                dve.wait_ge(dve_step, n.up())
                dve.tensor_tensor(tiles, tiles, denom[:, :].unsqueeze(2).to_broadcast([P, 8, P]), ALU.mult).then_inc(probs_ready, 1)

            def attention_out(i):
                dve.wait_ge(attended, i + 1)
                for g in range(2):
                    rows = slice(g * HD, (g + 1) * HD)
                    for c in range(2):
                        o = dve.tensor_copy(q[rows, :, bass.ds(i * P + c * CHUNK, CHUNK)],
                                            psum[rows, 6 + c, g * 256:(g + 1) * 256].rearrange("p (j t) -> p j t", t=CHUNK))
                        o.then_inc(pair3_read if g + c == 2 else dve_step, 1)
                for _ in range(3):
                    n.up()

            def gates(b0, z0, act0, into, after, attention=False):
                def step(i, last):
                    if attention:
                        softmax_shift(i)
                    ring_lo_of(b0 + 1, 2, i, z0 + 1, KB)
                    if attention:
                        softmax_scale(i)
                    if last:
                        after()
                    else:
                        ring_lo_of(b0 + 2, 2, i, z0 + 2)
                    merge(i, z0, act0, into)
                    if attention:
                        attention_out(i)
                per = 9 if attention else 0
                with dve.Fori(0, KD - 1) as i:
                    n.enter(i, 0, per)
                    step(i, False)
                n.leave(KD - 1)
                step(KD - 1, True)

            dve.wait_ge(alibi_in, 16)
            gates(B_GC, Z_GC, 10, 0, lambda: ring_lo_of(B_A, 0, 0, Z_A), attention=True)
            dve.wait_ge(zeroed, 3)

            def taps(dst, src, w, done):
                dve.tensor_scalar(dst, src[:, 2:], w(2), None, ALU.mult).then_inc(dve_step, 1)
                dve.wait_ge(dve_step, n.up())
                dve.scalar_tensor_tensor(out=dst, in0=src[:, 1:1 + S], scalar=w(1), in1=dst,
                                         op0=ALU.mult, op1=ALU.add).then_inc(dve_step, 1)
                dve.wait_ge(dve_step, n.up())
                dve.scalar_tensor_tensor(out=dst, in0=src[:, 0:S], scalar=w(0), in1=dst,
                                         op0=ALU.mult, op1=ALU.add).then_inc(done, 1)

            for j in range(KB):
                z, b, col = Z_A + 3 * j, B_A + 3 * j, C_A + 3 * j
                ring_lo_of(b + 1, 0, 0, z + 1)
                ring_lo_of(b + 2, 0, 0, z + 2)
                dve.wait_ge(act_z, 19 + j)
                dve.wait_ge(z_done, z + 2)
                dve.scalar_tensor_tensor(out=a_ch[:, 2:], in0=pair((z + 1) % 2), scalar=bias_sb[:, col + 1:col + 2],
                                         in1=a_c[:, :], op0=ALU.add, op1=ALU.mult).then_inc(dve_z, 1)
                dve.wait_ge(dve_z, 17 + 2 * j)
                taps(a_conv[:, :], a_ch, lambda tap: conv_a_sb[:, 3 * j + tap:3 * j + tap + 1], dve_step)
                dve.wait_ge(dve_step, n.up())
                ring_lo_of(b + 3, 0, 0, z + 3)
                dve.wait_ge(z_done, z + 3)
                dve.scalar_tensor_tensor(out=a_y[:, :], in0=pair(z % 2), scalar=bias_sb[:, col + 2:col + 3],
                                         in1=a_conv[:, :], op0=ALU.add, op1=ALU.mult).then_inc(dve_z, 1)
                dve.wait_ge(dve_z, 18 + 2 * j)
                split_y(j, a_y[:, :], KB + 1 + j)

            gates(B_GA, Z_GA, 22, 25, lambda: ring_lo_of(B_GB, 0, 0, Z_GB))
            for r in range(KB):
                split_y(r, q[:, r, :], 2 * KB + 1 + r)
            dve.wait_ge(merge_add, KD)

            def out_lo(first, wide_hi, wide_lo):
                for c in range(4):
                    cols = slice(c * P, (c + 1) * P)
                    lo(first + c, 0, 0, wide_lo[:, :, cols], wide_hi[:, :, cols])

            gates(B_GB, Z_GB, 30, 33, lambda: out_lo(B_OUT, wide_q_hi, wide_q_lo))
            for t in range(NT):
                cols = slice(t * P, (t + 1) * P)
                dve.wait_ge(m_hi, t + 1)
                dve.tensor_tensor(h_lo[:, :, cols], merged[:, :, cols], h_hi[:, :, cols].bitcast(F32), ALU.subtract).then_inc(m_lo, 1)
            out_lo(B_OUT + 4, wide_y_hi, wide_y_lo)
            for half in range(2):
                for t in range(NT):
                    if half == 0 and t % 2 == 0:
                        dve.wait_ge(xt_in[t // 2], 48)
                    dve.wait_ge(o_done, half * NT + t + 1)
                    bank = t % 8 if half == 0 else t % 4
                    dst = x1[:, t, half * HALF:(half + 1) * HALF]
                    dve.tensor_tensor(dst, dst, psum[:, bank, :], ALU.add).then_inc(x1_add, 1)
                    if half == 0:
                        continue
                    if t == 0:
                        dve.wait_ge(ffn_g_in, 16)
                    if t >= 2:
                        dve.wait_ge(turned, NT + t - 1)
                    dve.wait_ge(rs_ready, 2 * NT + t + 1)
                    dve.scalar_tensor_tensor(out=x_norm[:, t % 2, :], in0=x1[:, t, :], scalar=rs[:, 2 * NT + t:2 * NT + t + 1],
                                             in1=ffn_g_sb[:, :], op0=ALU.mult, op1=ALU.mult).then_inc(x_norm_ready, 1)
                    if t in (2, 3):
                        ring_lo_of(B_FF + t - 2, 0, 0, Z_FF + t - 2)
                    for r in ([t - 1] if t else []) + ([t] if t == NT - 1 else []):
                        dve.wait_ge(turned_hi, NT + r + 1)
                        cols = slice(r * P, (r + 1) * P)
                        dve.tensor_tensor(h_lo[:, :, cols], pair(2 + r % 2).rearrange("p (k n) -> p k n", n=P),
                                          h_hi[:, :, cols].bitcast(F32), ALU.subtract).then_inc(turned_lo, 1)

            def up_taps(dst, src, c, i):
                taps(dst[:, :], src, lambda tap: conv_f_sb[:, bass.ds(3 * c + tap + 12 * i, 1)], conv_done)

            def inner(r, i):
                dve.wait_ge(silu_done, 2 * i + r + 1)
                dve.tensor_tensor(conv_v[:, :], conv_v[:, :], conv_g[:, :], ALU.mult).then_inc(act_made, 1)
                dve.wait_ge(act_made, 2 * i + r + 1)
                dve.wait_ge(y_hi_done, 3 * KB + 2 * i + r + 1)
                dve.tensor_tensor(y_lo[:, r, :], conv_v[:, :], y_hi[:, r, :].bitcast(F32), ALU.subtract).then_inc(y_lo_done, 1)
                dve.wait_ge(y_lo_done, 3 * KB + 2 * i + r + 1)

            def last_val(i):
                dve.wait_ge(act_z, 38 + 4 * i)
                up_taps(conv_v, up_v, -1, i)
                dve.wait_ge(conv_done, 4 * i)
                inner(1, i - 1)

            def add_down(i):
                for t in range(NT):
                    dve.wait_ge(d_done, NT * i + t - NT + 1)
                    dve.tensor_tensor(x1[:, t, :], x1[:, t, :], pair(2 + t % 2), ALU.add).then_inc(x1_add, 1)

            def ffn(i, first):
                if not first:
                    ring_lo_of(B_FF, 6, i, Z_FF)
                    last_val(i)
                    ring_lo_of(B_FF + 1, 6, i, Z_FF + 1)
                dve.wait_ge(act_z, 39 + 4 * i)
                up_taps(conv_g, up_g, 0, i)
                ring_lo_of(B_FF + 2, 6, i, Z_FF + 2)
                if not first:
                    add_down(i)
                for c in range(2):
                    lo(B_FF + 3 + c, 6, i, wd_lo[:, c, :], wd_hi[:, c, :])
                ring_lo_of(B_FF + 5, 6, i, Z_FF + 3)
                dve.wait_ge(act_z, 40 + 4 * i)
                up_taps(conv_v, up_v, 1, i)
                dve.wait_ge(conv_done, 4 * i + 2)
                inner(0, i)
                dve.wait_ge(act_z, 41 + 4 * i)
                up_taps(conv_g, up_g, 2, i)

            ffn(0, True)
            with dve.Fori(1, FF_STEPS) as i:
                n.enter(i, 1, 8)
                ffn(i, False)
            n.leave(FF_STEPS - 1)
            last_val(FF_STEPS)
            add_down(FF_STEPS)

        @block.tensor
        def _(pe):
            def product(z, r_hi, r_lo, tiles, halves=(0, 1)):
                s = z % 2
                for k in range(tiles):
                    w = slice(k * P, (k + 1) * P)
                    for part, (weights, moving) in enumerate(((ring_hi, r_hi), (ring_hi, r_lo), (ring_lo, r_hi))):
                        for half in halves:
                            mm = pe.matmul(psum[:, 2 * s + half, :], weights[:, s, w],
                                           moving[:, k, half * HALF:(half + 1) * HALF],
                                           start=(k == 0 and part == 0), stop=(k == tiles - 1 and part == 2))
                return mm

            def rows_product(bank, t, a_hi, a_lo, wide_hi, wide_lo, tiles=KD):
                rows = slice(t * P, (t + 1) * P)
                for k in range(tiles):
                    for part, (a, w) in enumerate(((a_hi, wide_hi), (a_hi, wide_lo), (a_lo, wide_hi))):
                        mm = pe.matmul(psum[:, bank, :], a[:, k, rows], w[:, k, :],
                                       start=(k == 0 and part == 0), stop=(k == tiles - 1 and part == 2))
                return mm

            def turn_rows(dst, src):
                for k in range(KD):
                    mm = pe.transpose(dst[:, k * P:(k + 1) * P], src[:, k * P:(k + 1) * P], ident_sb[:, :])
                mm.then_inc(turned, 1)

            pe.wait_ge(c_in, 16 * 12)
            for step in range(NT + 1):
                if step < NT:
                    pe.wait_ge(x_norm_ready, step + 1)
                    if step >= 2:
                        pe.wait_ge(dve_z, step - 1)
                    turn_rows(pair(step % 2), x_in[:, step % 4, :])
                t = step - 1
                if t >= 0:
                    if t == 0:
                        pe.wait_ge(w_lo, 4)
                    pe.wait_ge(dve_z, t + 1)
                    if t >= 2:
                        pe.wait_ge(sv_biased, t - 1)
                    rows_product(4 + t % 2, t, h_hi, h_lo, wide_y_hi, wide_y_lo).then_inc(sv_done, 1)

            def ring(z, before):
                pe.wait_ge(w_lo, z + 5)
                if before:
                    pe.wait_ge(act_z, before)
                product(z, h_hi, h_lo, KD).then_inc(z_done, 1)

            def head_sums(m):
                pe.wait_ge(qk_sq, m + 1)
                if m:
                    pe.wait_ge(pair2_read, m)
                else:
                    pe.wait_ge(sv_biased, NT)
                for half in range(2):
                    mm = pe.matmul(psum[:, 4 + half, :], ones_sb[:, :], square[:, half * HALF:(half + 1) * HALF],
                                   start=True, stop=True)
                mm.then_inc(qk_sum, 1)

            def turn_v(half):
                pe.wait_ge(act_z, 2)
                pe.wait_ge(zeroed, 2)
                if half:
                    pe.wait_ge(pair3_read, half)
                for c in range(8):
                    first = (8 * half + c) * CHUNK
                    mm = pe.transpose(pair(3)[:, c * P:(c + 1) * P], v_pad[:, first:first + P], ident_sb[:, :])
                mm.then_inc(v_turned, 1)

            def mix(g):
                if g == 0:
                    pe.wait_ge(vhat_ready, NT)
                    pe.wait_ge(masked, 1)
                pe.wait_ge(pair3_read, 2 + g)
                for t in range(NT):
                    mm = pe.matmul(pair(3)[:, t * P:(t + 1) * P], vhat[:, t, g * P:(g + 1) * P], sgu_wt_sb[:, g, :],
                                   start=True, stop=True)
                mm.then_inc(mixed, 1)

            ring(Z_K, 0)
            ring(Z_V, 0)
            head_sums(0)
            ring(Z_Q, 1)
            turn_v(0)
            ring(Z_Q + 1, 2)
            head_sums(1)
            turn_v(1)
            ring(Z_Q + 2, 3)
            head_sums(2)
            ring(Z_Q + 3, 4)
            head_sums(3)
            ring(Z_U, 5)
            head_sums(4)
            for g in range(SG):
                if g:
                    ring(Z_U + g, 5 + g)
                mix(g)

            def score_two(i):
                pe.wait_ge(staged, 3 * i + 3)
                pe.wait_ge(pair2_read, 5 + i)
                for c in range(2):
                    for g in range(2):
                        for j in range(2):
                            o = (2 * g + j) * P
                            mm = pe.matmul(psum[:, 4 + c, o:o + P],
                                           q_st[:, g, c, 2 * j:2 * j + 2, :].rearrange("p j t -> p (j t)"),
                                           k_pad[:, bass.ds(i * P + c * CHUNK, P)], start=True, stop=True)
                mm.then_inc(scores, 1)

            def turn_probs(i):
                pe.wait_ge(probs_ready, i + 1)
                pe.wait_ge(pair3_read, 2 + SG + i)
                for c in range(8):
                    mm = pe.transpose(pair(3)[:, c * P:(c + 1) * P], probs[:, c * P:(c + 1) * P], ident_sb[:, :])
                mm.then_inc(probs_turned, 1)

            def attend(i):
                pe.wait_ge(probs_t_ready, i + 1)
                for c in range(2):
                    for g in range(2):
                        mm = pe.matmul(psum[:, 6 + c, g * 256:(g + 1) * 256], v_st[:, c, :],
                                       probs_t[:, c, g * 256:(g + 1) * 256], start=True, stop=True)
                mm.then_inc(attended, 1)

            def gates(b0, z0, act0, dve0, y0, attention=False):
                with pe.Fori(0, KD) as i:
                    if attention:
                        score_two(i)
                    pe.wait_ge(w_lo, b0 + 1 + 2 * i)
                    pe.wait_ge(act_z, act0 + i)
                    product(z0, h_hi, h_lo, KD).then_inc(z_done, 1)
                    if attention:
                        turn_probs(i)
                    pe.wait_ge(w_lo, b0 + 2 + 2 * i)
                    pe.wait_ge(dve_z, dve0 + i)
                    pe.wait_ge(y_lo_done, y0)
                    product(z0 + 1, y_hi, y_lo, KB).then_inc(z_done, 1)
                    if attention:
                        attend(i)

            pe.wait_ge(qk_ready, 5)
            gates(B_GC, Z_GC, 10, 8, SG, attention=True)
            with pe.Fori(0, 2) as i:
                for c, waits in enumerate((
                        ((act_z, 18 + 2 * i), (dve_z, 15 + 4 * i)), ((dve_z, 16 + 4 * i),), ((act_z, 19 + 2 * i),),
                        ((dve_z, 17 + 4 * i),), ((dve_z, 18 + 4 * i),), ((act_z, 20 + 2 * i),))):
                    pe.wait_ge(w_lo, B_A + c + 1 + 6 * i)
                    for s, v in waits:
                        pe.wait_ge(s, v)
                    product(Z_A + c, h_hi, h_lo, KD).then_inc(z_done, 1)
            pe.wait_ge(dve_z, 23)
            gates(B_GA, Z_GA, 22, 24, 2 * KB)
            gates(B_GB, Z_GB, 30, 32, 3 * KB)

            pe.wait_ge(act_z, 38)
            pe.wait_ge(dve_z, 40)
            pe.wait_ge(pair3_read, 2 + SG + NT)
            pe.wait_ge(w_lo, B_OUT + 4)
            for t in range(NT):
                pe.wait_ge(m_lo, t + 1)
                rows_product(t, t, h_hi, h_lo, wide_q_hi, wide_q_lo).then_inc(o_done, 1)
            pe.wait_ge(w_lo, B_OUT + 8)

            def turn_x1(t):
                pe.wait_ge(x_norm_ready, NT + t + 1)
                if t < 2:
                    pe.wait_ge(x1_add, 6 + 2 * t)
                else:
                    pe.wait_ge(turned_lo, t - 1)
                turn_rows(pair(2 + t % 2), x_norm[:, t % 2, :])

            for t in range(NT):
                pe.wait_ge(x1_add, t + 1 if t < 4 else NT + t - 3)
                rows_product(t % 4, t, h_hi, h_lo, wide_y_hi, wide_y_lo).then_inc(o_done, 1)
                if t:
                    turn_x1(t - 1)

            def up(c, block, i, before):
                pe.wait_ge(w_lo, B_FF + block + 1 + 6 * i)
                pe.wait_ge(act_z, before + 4 * i)
                product(Z_FF + c, h_hi, h_lo, KD).then_inc(z_done, 1)

            def down(i):
                pe.wait_ge(y_lo_done, 3 * KB + 2 * i)
                pe.wait_ge(w_lo, B_FF + 6 * i - 1)
                for t in range(NT):
                    pe.wait_ge(x1_add, NT - 1 + NT * i + t)
                    rows = slice(t * P, (t + 1) * P)
                    for r in range(2):
                        for part, (a, w) in enumerate(((y_hi, wd_hi), (y_hi, wd_lo), (y_lo, wd_hi))):
                            for half in range(2):
                                mm = pe.matmul(psum[:, 4 + 2 * (t % 2) + half, :], a[:, r, rows],
                                               w[:, r, half * HALF:(half + 1) * HALF],
                                               start=(r == 0 and part == 0), stop=(r == 1 and part == 2))
                    mm.then_inc(d_done, 1)

            pe.wait_ge(w_lo, B_FF + 2)
            pe.wait_ge(x1_add, NT + 6)
            pe.wait_ge(turned_lo, 4)
            product(Z_FF, h_hi, h_lo, KD, (0,))
            turn_x1(NT - 1)
            pe.wait_ge(x1_add, 2 * NT)
            product(Z_FF + 1, h_hi, h_lo, KD, (0,))
            pe.wait_ge(turned_lo, NT)
            product(Z_FF, h_hi, h_lo, KD, (1,)).then_inc(z_done, 1)
            product(Z_FF + 1, h_hi, h_lo, KD, (1,)).then_inc(z_done, 1)
            up(2, 2, 0, 39)
            up(3, 5, 0, 40)
            with pe.Fori(1, FF_STEPS) as i:
                up(0, 0, i, 37)
                down(i)
                up(1, 1, i, 38)
                up(2, 2, i, 39)
                up(3, 5, i, 40)
            down(FF_STEPS)


def blocks(w, cols):
    import numpy as np

    k = w.shape[0] // P
    w = w[:, cols].reshape(k, P, len(cols) // P, P)
    return np.ascontiguousarray(w.transpose(2, 1, 0, 3)).reshape(len(cols) // P, P, k * P)


def kernel(**inputs):
    import concourse.bacc as bacc
    import numpy as np
    from concourse.bass_utils import run_bass_kernel_spmd

    a = {k: np.asarray(v) for k, v in inputs.items()}
    f = np.float32
    ab, ac, ah, qo, ko, vo, uo, so, go = 0, 512, 1024, 1536, 2048, 2176, 2304, 2816, 3328
    tile = np.arange(P)
    half = np.arange(HD)
    cols = [so + np.arange(BR), ko + tile, vo + tile]
    cols += [np.concatenate([qo + j * HD + half, qo + (4 + j) * HD + half]) for j in range(4)]
    cols += [uo + np.arange(BR), go + 2 * D + np.arange(D)]
    for j in range(KB):
        cols += [ac + j * P + tile, ah + j * P + tile, ab + j * P + tile]
    cols += [go + np.arange(D), go + D + np.arange(D)]
    cols = np.concatenate(cols)
    bin_ = a["b_in"][0]
    heads = np.concatenate([np.concatenate([j * HD + half, (4 + j) * HD + half]) for j in range(4)])
    wb = a["w_branch"][0]
    every = np.arange(D)
    ff = np.concatenate([np.concatenate([r * P + tile, FF_TILES * P + r * P + tile]) for r in range(FF_TILES)])
    row, key = np.arange(P), np.arange(P)
    table = np.zeros((P, 2, 2, 2, P), f)
    for g in range(2):
        for j in range(2):
            head = 4 * g + 2 * j + row // CHUNK
            slope = 2.0 ** -(head + 1.0)
            table[:, :, g, j, :] = (-slope[:, None] * np.abs(CHUNK + row % CHUNK - key[:, None]).T)[:, None, :]
    table[:, 0, :, :, 0:CHUNK] = -1e30
    head_ones = (row[:, None] // HD == row[None, :] // HD).astype(f)
    arrays = {
        "x": a["x"][0],
        "w_in": blocks(a["w_in"][0], cols),
        "bias": np.ascontiguousarray(bin_[cols].reshape(-1, P).T),
        "w_branch": np.concatenate([blocks(wb[2], every), blocks(wb[0], every), blocks(wb[1][heads], every)]),
        "w_out": blocks(a["w_out"][0], every),
        "w_up": blocks(a["w_up"][0], ff),
        "w_down": a["w_down"][0].reshape(FF_TILES, P, D),
        "mix_g": a["mix_norm_g"],
        "ffn_g": a["ffn_norm_g"],
        "sv_bias": bin_[None, so:so + BR],
        "sgu_wt": np.ascontiguousarray(a["sgu_w"][0].transpose(2, 0, 1)).reshape(P, SG * P),
        "sgu_b": a["sgu_b"][0].reshape(1, SG * P),
        "sgu_g": np.ascontiguousarray(a["sgu_norm_g"][0].reshape(SG, P).T),
        "conv_a": np.ascontiguousarray(a["conv_a_w"][0].reshape(3, KB, P).transpose(2, 1, 0)).reshape(P, KB * 3),
        "conv_f": np.ascontiguousarray(a["conv_f_w"][0][:, ff].reshape(3, 2 * FF_TILES, P).transpose(2, 1, 0)).reshape(P, -1),
        "q_gain": np.tile(a["q_norm_g"][0], 2)[:, None],
        "k_gain": np.tile(a["k_norm_g"][0], 2)[:, None],
        "sink": np.ascontiguousarray(a["attn_sink"][0].reshape(2, 2, 2).transpose(2, 0, 1)).reshape(2, 4),
        "alibi": table.reshape(P, 2 * HALF),
        "ident": np.eye(P, dtype=f),
        "head_ones": head_ones,
    }
    nc = bacc.Bacc("TRN2", target_bir_lowering=False, num_devices=1)
    arrays = {f"in_{k}": np.ascontiguousarray(v) for k, v in arrays.items()}
    args = [nc.dram_tensor(k, v.shape, mybir.dt.from_np(v.dtype), kind="ExternalInput").ap() for k, v in arrays.items()]
    out = nc.dram_tensor("out", (S, D), F32, kind="ExternalOutput").ap()
    hybrid_layer(nc, *args, out)
    r = run_bass_kernel_spmd(nc, [arrays], core_ids=[0])
    return r.results[0]["out"].reshape(1, S, D)
```

```python
from contextlib import ExitStack

import concourse.bass as bass
from concourse import mybir

F32 = mybir.dt.float32
F32R = mybir.dt.float32r
ALU = mybir.AluOpType
ACT = mybir.ActivationFunctionType
AX_X = mybir.AxisListType.X

P = 128
S = 1024
D = 1024
KD = D // P
NT = S // P
HALF = 512
BR = 512
KB = BR // P
HD = 64
CHUNK = 64
SG = 4
FIRST_BANKS = (0, 1, 4, 5, 2, 3, 6, 7)
FF_TILES = 22
FF_STEPS = FF_TILES // 2
EPS = 1e-6
SBUF_BYTES = 212800

B_SV, B_K, B_V, B_Q, B_U = 0, 4, 5, 6, 10
B_GC, B_A, B_GA, B_GB, B_OUT, B_FF = 14, 30, 42, 58, 74, 82
C_SV, C_K, C_V, C_Q, C_U, C_GC, C_A, C_GA, C_GB = 0, 4, 5, 6, 10, 14, 22, 34, 42
Z_K, Z_V, Z_Q, Z_U, Z_GC, Z_A, Z_GA, Z_GB, Z_FF = 0, 1, 2, 6, 10, 26, 38, 54, 70


def squared_at(step):
    return ([("x", step + 1)] if step + 1 < NT else []) + ([("s_v", step - 2)] if 0 <= step - 2 < NT else [])


class Count:

    def __init__(self):
        self.n, self.shift = 0, 0

    def up(self):
        self.n += 1
        return self.n + self.shift

    def enter(self, i, first, per):
        self.start, self.per, self.shift = self.n, per, (i - first) * per

    def leave(self, trips):
        assert self.n - self.start == self.per, (self.n - self.start, self.per)
        self.n, self.shift = self.start + self.per * trips, 0


def hybrid_layer(nc, x, w_in, bias, w_branch, w_out, w_up, w_down, mix_g, ffn_g, sv_bias, sgu_wt,
                 sgu_b, sgu_g, conv_a, conv_f, q_gain, k_gain, sink, alibi, ident, head_ones, out):
    with ExitStack() as ctx:
        base = nc.sbuf_base
        ctx.enter_context(nc.sbuf_tensor("arena", [P, SBUF_BYTES // 4], F32))

        def at(name, offset, shape, dt=F32):
            size = 4
            for n in shape[1:]:
                size *= n
            assert offset + size <= SBUF_BYTES - 32, (name, offset + size)
            start = (base + 31) // 32 * 32
            return nc.alloc_sbuf_tensor_at(name, shape, dt, offset=start + offset)

        K1 = 1024
        R1, MG, YB, QR = 0, 64 * K1, 96 * K1, 128 * K1
        RING = QR + 46336
        TMP = RING + 24 * K1
        CST = TMP + 8 * K1

        h_hi = at("h_hi", R1, [P, KD, S], F32R)
        h_lo = at("h_lo", R1 + 32 * K1, [P, KD, S], F32R)
        merged = at("merged", MG, [P, KD, S])
        x1 = at("x1", MG, [P, NT, D])
        vhat = at("vhat", MG, [P, NT, BR])
        x_in = at("x_in", MG + 16 * K1, [P, 4, D])
        raw_k = at("raw_k", MG + 16 * K1, [P, S])
        square = at("square", MG + 20 * K1, [P, S])
        meansq_qk = at("meansq_qk", MG + 24 * K1, [P, 5, 2 * NT])
        rs_qk = at("rs_qk", MG + 25 * K1, [P, 5, 2 * NT])
        y_hi = at("y_hi", YB, [P, KB, S], F32R)
        y_lo = at("y_lo", YB + 16 * K1, [P, KB, S], F32R)
        wide_y_hi = at("wide_y_hi", YB, [P, KD, HALF], F32R)
        wide_y_lo = at("wide_y_lo", YB + 16 * K1, [P, KD, HALF], F32R)
        q = at("q", QR, [P, 4, S])
        raw_sv = at("raw_sv", QR, [P, 4, D])
        v_win = at("v_win", QR + 16384, [P, 16, P])
        k_pad = at("k_pad", QR + 24576, [P, CHUNK + S])
        alibi_sb = at("alibi_sb", QR + 28928, [P, 2, HALF])
        q_st = at("q_st", QR + 33024, [P, 2, 2, 4, CHUNK])
        v_st = at("v_st", QR + 37120, [P, 2, P])
        probs = at("probs", QR + 38144, [P, 2 * HALF])
        probs_t = at("probs_t", QR + 42240, [P, 2, HALF])
        v_pad = at("v_pad", QR + 28928, [P, CHUNK + S])
        mix_g_sb = at("mix_g_sb", QR + 38144, [P, D])
        rs_wide = at("rs_wide", QR + 38144, [P, 2 * NT, HD])
        row_sb = at("row_sb", QR + 42240, [P, BR])
        sgu_wt_sb = at("sgu_wt_sb", QR + 42240 + 2048, [P, SG, P])
        a_c = at("a_c", QR + 16384, [P, S])
        a_conv = at("a_conv", QR + 20480, [P, S])
        a_ch = at("a_ch", QR + 24576, [P, 2 + S])
        a_y = at("a_y", QR + 28928, [P, S])
        wide_q_hi = at("wide_q_hi", QR, [P, KD, HALF], F32R)
        wide_q_lo = at("wide_q_lo", QR + 16384, [P, KD, HALF], F32R)
        x_norm = at("x_norm", QR + 33024, [P, 2, D])
        ffn_g_sb = at("ffn_g_sb", QR + 41216, [P, D])
        wd_hi = at("wd_hi", QR, [P, 2, D], F32R)
        wd_lo = at("wd_lo", QR + 8192, [P, 2, D], F32R)
        up_g = at("up_g", QR + 16384, [P, 2 + S])
        up_v = at("up_v", QR + 20512, [P, 2 + S])
        conv_g = at("conv_g", QR + 24640, [P, S])
        conv_v = at("conv_v", QR + 28736, [P, S])
        wd_last_hi = at("wd_last_hi", QR + 32832, [P, 2, D], F32R)
        wd_last_lo = at("wd_last_lo", RING + 24 * K1, [P, 2, D], F32R)
        raw = at("raw", RING, [P, 2, D])
        ring_hi = at("ring_hi", RING + 8 * K1, [P, 2, D], F32R)
        ring_lo = at("ring_lo", RING + 16 * K1, [P, 2, D], F32R)
        gate = at("gate", TMP, [P, S])
        prod = at("prod", TMP + 4 * K1, [P, S])
        place = [CST]

        def small(name, shape):
            t = at(name, place[0], shape)
            n = 4
            for m in shape[1:]:
                n *= m
            place[0] += (n + 31) // 32 * 32
            return t

        ident_sb = small("ident_sb", [P, P])
        ones_sb = small("ones_sb", [P, P])
        bias_sb = small("bias_sb", [P, 50])
        conv_f_sb = small("conv_f_sb", [P, 2 * FF_TILES * 3])
        conv_a_sb = small("conv_a_sb", [P, KB * 3])
        q_gain_sb = small("q_gain_sb", [P, 1])
        q_scale_sb = small("q_scale_sb", [P, 1])
        k_gain_sb = small("k_gain_sb", [P, 1])
        sgu_g_sb = small("sgu_g_sb", [P, SG])
        sink_sb = small("sink_sb", [P, 8])
        peak = small("peak", [P, 8])
        sink_e = small("sink_e", [P, 8])
        denom = small("denom", [P, 8])
        power = small("power", [P, 2 * NT])
        sumsq = small("sumsq", [P, 3 * NT])
        meansq = small("meansq", [P, 3 * NT])
        rs = small("rs", [P, 3 * NT])

        psum = ctx.enter_context(nc.psum_tensor("psum", [P, 8, HALF], F32))

        def pair(n):
            return psum[:, 2 * n:2 * n + 2, :].rearrange("p a b -> p (a b)")

        def sem(name):
            return ctx.enter_context(nc.semaphore(name))

        raw_in = [sem(f"raw_in{n}") for n in range(2)]
        sv_in = [sem(f"sv_in{n}") for n in range(4)]
        xt_in = [sem(f"xt_in{n}") for n in range(4)]
        norm_in = sem("norm_in")
        c_in = sem("c_in")
        alibi_in = sem("alibi_in")
        row_in = sem("row_in")
        ffn_g_in = sem("ffn_g_in")
        out_done = sem("out_done")
        w_hi = sem("w_hi")
        w_lo = sem("w_lo")
        z_done = sem("z_done")
        act_z = sem("act_z")
        dve_z = sem("dve_z")
        pair2_read = sem("pair2_read")
        pair3_read = sem("pair3_read")
        squared = sem("squared")
        rs_ready = sem("rs_ready")
        pool_step = sem("pool_step")
        zeroed = sem("zeroed")
        x_norm_ready = sem("x_norm_ready")
        turned = sem("turned")
        turned_hi = sem("turned_hi")
        turned_lo = sem("turned_lo")
        sv_done = sem("sv_done")
        sv_biased = sem("sv_biased")
        sv_gelu = sem("sv_gelu")
        vhat_ready = sem("vhat_ready")
        qk_sq = sem("qk_sq")
        qk_sum = sem("qk_sum")
        qk_mean = sem("qk_mean")
        qk_rs = sem("qk_rs")
        qk_turned = sem("qk_turned")
        v_ready = sem("v_ready")
        v_turned = sem("v_turned")
        u_ready = sem("u_ready")
        mixed = sem("mixed")
        y_ready = sem("y_ready")
        y_hi_done = sem("y_hi_done")
        y_lo_done = sem("y_lo_done")
        staged = sem("staged")
        v_staged = sem("v_staged")
        scores = sem("scores")
        shifted = sem("shifted")
        exps = sem("exps")
        probs_ready = sem("probs_ready")
        probs_turned = sem("probs_turned")
        probs_t_ready = sem("probs_t_ready")
        attended = sem("attended")
        ac_ready = sem("ac_ready")
        m_hi = sem("m_hi")
        m_lo = sem("m_lo")
        o_done = sem("o_done")
        x1_add = sem("x1_add")
        conv_done = sem("conv_done")
        silu_done = sem("silu_done")
        act_made = sem("act_made")
        d_done = sem("d_done")
        masked = sem("masked")
        merge_add = sem("merge_add")
        dve_step = sem("dve_step")

        block = ctx.enter_context(nc.Block())

        @block.sync
        def _(sp):
            def load(const, per, i, src, width=D):
                slot = const % 2
                if const >= B_Q:
                    sp.wait_ge(w_lo, const - 1 + per * i)
                sp.dma_start(raw[:, slot, 0:width], src).then_inc(raw_in[slot], 16)

            def load_sv(b):
                sp.dma_start(raw_sv[:, b, :], w_in[C_SV + b]).then_inc(sv_in[b], 16)

            def load_x(t):
                sp.dma_start(x_in[:, t % 4, :], x[t * P:(t + 1) * P, :]).then_inc(xt_in[t % 4], 16)

            load_x(0)
            sp.dma_start(ident_sb[:, :], ident).then_inc(norm_in, 16)
            sp.dma_start(mix_g_sb[:, :], mix_g.to_broadcast([P, D])).then_inc(norm_in, 16)
            load_sv(0)
            load_x(1)
            for b in range(1, 4):
                load_sv(b)
            load_x(2)
            sp.dma_start(row_sb[:, :], sv_bias.to_broadcast([P, BR])).then_inc(row_in, 16)
            load_x(3)
            for dst, src in ((ones_sb, head_ones), (bias_sb, bias), (conv_f_sb, conv_f), (conv_a_sb, conv_a),
                             (q_gain_sb, q_gain), (k_gain_sb, k_gain), (sgu_g_sb, sgu_g),
                             (sgu_wt_sb, sgu_wt)):
                full = dst[:, :, :].rearrange("p a b -> p (a b)") if dst is sgu_wt_sb else dst[:, :]
                sp.dma_start(full, src).then_inc(c_in, 16)
            for b in range(2):
                sp.dma_start(sink_sb[b * HD:(b + 1) * HD, 0:4], sink[b:b + 1, :].to_broadcast([HD, 4])).then_inc(c_in, 16)
            for c in (B_K, B_V):
                load(c, 0, 0, w_in[c])
            for t in range(4, NT):
                sp.wait_ge(turned, t - 3)
                load_x(t)
            sp.wait_ge(sv_biased, NT)
            sp.dma_start(row_sb[:, :], sgu_b.to_broadcast([P, BR])).then_inc(row_in, 16)
            for c in range(6, 10):
                load(c, 0, 0, w_in[c])
            sp.wait_ge(pair3_read, 2)
            sp.dma_start(alibi_sb[:, :, :].rearrange("p a b -> p (a b)"), alibi).then_inc(alibi_in, 16)
            for c in range(10, 14):
                load(c, 0, 0, w_in[c])

            def gate_loads(b0, c0, n):
                with sp.Fori(0, KD) as i:
                    load(b0, 2, i, w_in[c0 + i])
                    load(b0 + 1, 2, i, w_branch[n * KD + i], KB * P)

            gate_loads(B_GC, C_GC, 0)
            with sp.Fori(0, 2) as i:
                for c in range(6):
                    load(B_A + c, 6, i, w_in[C_A + c + 6 * i])
            gate_loads(B_GA, C_GA, 1)
            gate_loads(B_GB, C_GB, 2)
            for c in range(2 * KB):
                load(B_OUT + c, 0, 0, w_out[c])
            sp.wait_ge(m_lo, NT)
            for n in range(4):
                sp.dma_start(x1[:, 2 * n:2 * n + 2, :], x[2 * n * P:(2 * n + 2) * P, :].rearrange("(t p) d -> p t d", p=P)).then_inc(xt_in[n], 16)
            sp.dma_start(ffn_g_sb[:, :], ffn_g.to_broadcast([P, D])).then_inc(ffn_g_in, 16)
            with sp.Fori(0, FF_STEPS) as i:
                load(B_FF, 6, i, w_up[4 * i])
                load(B_FF + 1, 6, i, w_up[4 * i + 1])
                load(B_FF + 2, 6, i, w_up[4 * i + 2])
                load(B_FF + 3, 6, i, w_down[2 * i])
                load(B_FF + 4, 6, i, w_down[2 * i + 1])
                load(B_FF + 5, 6, i, w_up[4 * i + 3])
            for t in range(NT):
                sp.wait_ge(x1_add, 2 * NT + NT * (FF_STEPS - 1) + t + 1)
                sp.dma_start(out[t * P:(t + 1) * P, :], x1[:, t, :]).then_inc(out_done, 16)
            sp.wait_ge(out_done, 16 * NT)

        @block.gpsimd
        def _(pool):
            n = Count()
            pool.memset(power[:, :], -0.5).then_inc(pool_step, 1)
            pool.wait_ge(pool_step, n.up())

            def row_rs(col, need, width):
                pool.wait_ge(squared, need)
                pool.tensor_scalar(meansq[:, col:col + 1], sumsq[:, col:col + 1], 1.0 / width, EPS,
                                   ALU.mult, ALU.add).then_inc(pool_step, 1)
                pool.wait_ge(pool_step, n.up())
                pool.tensor_tensor(rs[:, col:col + 1], meansq[:, col:col + 1], power[:, 0:1],
                                   ALU.pow).then_inc(rs_ready, 1)

            def first_lo(b, dst, src, part):
                pool.wait_ge(w_hi, b + 1)
                pool.tensor_tensor(dst, src, part.bitcast(F32), ALU.subtract).then_inc(w_lo, 1)

            order = 0
            for step in range(-1, NT + 2):
                for kind, t in squared_at(step):
                    order += 1
                    row_rs(t if kind == "x" else NT + t, order, D if kind == "x" else BR)
                if step == 0:
                    first_lo(1, wide_y_lo[:, :, P:2 * P], raw_sv[:, 1, :].rearrange("p (k n) -> p k n", n=P),
                             wide_y_hi[:, :, P:2 * P])
                if step in (5, 7):
                    b = B_K + (step - 5) // 2
                    first_lo(b, ring_lo[:, b % 2, :], raw[:, b % 2, :], ring_hi[:, b % 2, :])
            pool.wait_ge(c_in, 16 * 10)
            pool.wait_ge(rs_ready, 2 * NT)
            pool.memset(sgu_wt_sb[CHUNK:P, :, 0:CHUNK], 0.0).then_inc(masked, 1)
            pool.wait_ge(masked, 1)
            pool.memset(v_pad[:, 0:CHUNK], 0.0).then_inc(zeroed, 1)
            pool.memset(k_pad[:, 0:CHUNK], 0.0).then_inc(zeroed, 1)
            def head_rs(m):
                pool.wait_ge(qk_mean, m + 1)
                pool.tensor_tensor(rs_qk[:, m, :], meansq_qk[:, m, :], power[:, :], ALU.pow).then_inc(pool_step, 1)
                pool.wait_ge(pool_step, n.up())
                if m:
                    pool.wait_ge(qk_turned, m)
                pool.tensor_copy(rs_wide[:, :, :], rs_qk[:, m, :].unsqueeze(2).to_broadcast([P, 2 * NT, HD])).then_inc(qk_rs, 1)

            head_rs(0)
            pool.wait_ge(qk_rs, 1)
            pool.wait_ge(pair3_read, 2)
            for g in range(2):
                rows = slice((1 - g) * HD, (2 - g) * HD)
                pool.memset(q_st[rows, g, :, :, :].rearrange("p c j t -> p (c j t)"), 0.0).then_inc(pool_step, 1)
                pool.wait_ge(pool_step, n.up())
            for m in range(1, 5):
                head_rs(m)
            pool.wait_ge(qk_rs, 5)
            pool.wait_ge(pair2_read, 5)

            def stage(i):
                for g in range(2):
                    rows = slice(g * HD, (g + 1) * HD)
                    pool.tensor_copy(q_st[rows, g, :, :, :], q[rows, :, bass.ds(i * P, P)].rearrange("p j (c t) -> p c j t", t=CHUNK)).then_inc(staged, 1)
                    pool.wait_ge(staged, 2 * i + g + 1)

            def stage_v(i):
                pool.tensor_copy(v_st[:, :, :], v_win[:, bass.ds(2 * i, 2), :]).then_inc(v_staged, 1)

            stage(0)
            stage_v(0)
            with pool.Fori(1, NT) as i:
                pool.wait_ge(scores, i)
                stage(i)
                pool.wait_ge(attended, i)
                stage_v(i)
            pool.wait_ge(attended, NT)
            pool.memset(a_ch[:, 0:2], 0.0).then_inc(zeroed, 1)
            for t in range(NT):
                row_rs(2 * NT + t, 2 * NT + t + 1, D)
            pool.wait_ge(o_done, NT)
            pool.memset(up_g[:, 0:2], 0.0).then_inc(zeroed, 1)
            pool.memset(up_v[:, 0:2], 0.0).then_inc(zeroed, 1)

        @block.scalar
        def _(act):
            def hi(const, per, i, dst, tiles=KD):
                slot = const % 2
                if const < B_K:
                    act.wait_ge(sv_in[const], 16)
                    src = raw_sv[:, const, :]
                else:
                    act.wait_ge(raw_in[slot], 16 * ((const - B_K) // 2 + 1) + 8 * per * i)
                    src = raw[:, slot, 0:tiles * P]
                if len(dst.shape) == 3:
                    src = src.rearrange("p (k n) -> p k n", n=dst.shape[2])
                act.activation(dst, src, ACT.Copy).then_inc(w_hi, 1)

            def ring_hi_of(const, per, i, z, per_z, tiles=KD):
                if z >= 2:
                    act.wait_ge(z_done, z - 1 + per_z * i)
                hi(const, per, i, ring_hi[:, z % 2, 0:tiles * P], tiles)

            def rows_squared(src, col):
                act.activation(gate[:, 0:src.shape[1]], src, ACT.Square,
                               accum_out=sumsq[:, col:col + 1]).then_inc(squared, 1)

            n_squared = 0
            for step in range(-1, NT + 2):
                t = step - 1
                if 0 <= t < NT:
                    act.wait_ge(turned, t + 1)
                    act.activation(h_hi[:, :, t * P:(t + 1) * P],
                                   pair(t % 2).rearrange("p (k n) -> p k n", n=P), ACT.Copy).then_inc(turned_hi, 1)
                if step == 1:
                    for b in range(1, 4):
                        hi(b, 0, 0, wide_y_hi[:, :, b * P:(b + 1) * P])
                for kind, t in squared_at(step):
                    if kind == "x":
                        act.wait_ge(xt_in[t % 4], 16 * (t // 4 + 1))
                        rows = x_in[:, t % 4, :]
                    else:
                        rows = vhat[:, t, :]
                        act.wait_ge(sv_biased, t + 1)
                        act.activation(rows, rows, ACT.Gelu_apprx_tanh).then_inc(sv_gelu, 1)
                        act.wait_ge(sv_gelu, t + 1)
                    if n_squared:
                        act.wait_ge(squared, n_squared)
                    rows_squared(rows, t if kind == "x" else NT + t)
                    n_squared += 1
                if step == -1:
                    hi(0, 0, 0, wide_y_hi[:, :, 0:P])
                if step in (4, 5):
                    ring_hi_of(step, 0, 0, step - 4, 0)

            def evac(z, dst, func=ACT.Identity, col=0):
                act.wait_ge(z_done, z + 1)
                return act.activation(dst, pair(z % 2), func, bias=bias_sb[:, col:col + 1])

            def qk_square(n):
                if n:
                    act.wait_ge(qk_sum, n)
                act.activation(square[:, :], raw_k[:, :] if n == 0 else q[:, n - 1, :], ACT.Square).then_inc(qk_sq, 1)

            act.wait_ge(c_in, 16 * 10)
            act.wait_ge(squared, 2 * NT)
            evac(Z_K, raw_k[:, :], col=C_K).then_inc(act_z, 1)
            ring_hi_of(B_Q, 0, 0, Z_Q, 0)
            act.wait_ge(act_z, 1)
            qk_square(0)
            evac(Z_V, v_pad[:, CHUNK:], col=C_V).then_inc(act_z, 1)
            ring_hi_of(B_Q + 1, 0, 0, Z_Q + 1, 0)
            for n in range(4):
                evac(Z_Q + n, q[:, n, :], col=C_Q + n).then_inc(act_z, 1)
                ring_hi_of(B_Q + n + 2, 0, 0, Z_Q + n + 2, 0)
                act.wait_ge(act_z, 3 + n)
                qk_square(n + 1)
            for n in range(SG):
                if n:
                    act.wait_ge(y_ready, n)
                if n == SG - 1:
                    ring_hi_of(B_GC, 0, 0, Z_GC, 0)
                evac(Z_U + n, gate[:, :], ACT.Gelu_apprx_tanh, C_U + n).then_inc(act_z, 1)
                if n < 2:
                    ring_hi_of(B_U + n + 2, 0, 0, Z_U + n + 2, 0)
                act.wait_ge(y_ready, n + 1)
                act.activation(y_hi[:, n, :], prod[:, :], ACT.Copy).then_inc(y_hi_done, 1)

            def gates(b0, z0, c0, dve0, after=None, before=None, attention=False):
                def step(i, last):
                    ring_hi_of(b0 + 1, 2, i, z0 + 1, 2, KB)
                    if attention:
                        act.wait_ge(shifted, 2 * i + 2)
                        act.activation(probs[:, :], probs[:, :], ACT.Exp).then_inc(exps, 1)
                        act.activation(sink_e[:, :], sink_e[:, :], ACT.Exp).then_inc(exps, 1)
                    if last and before:
                        before()
                    act.wait_ge(z_done, z0 + 1 + 2 * i)
                    act.wait_ge(dve_z, dve0 + i)
                    act.activation(gate[:, :], pair(0), ACT.Sigmoid, bias=bias_sb[:, bass.ds(c0 + i, 1)]).then_inc(act_z, 1)
                    if attention:
                        act.wait_ge(probs_turned, i + 1)
                        act.activation(probs_t[:, :, :].rearrange("p a b -> p (a b)"), pair(3), ACT.Copy).then_inc(probs_t_ready, 1)
                    if not last:
                        ring_hi_of(b0 + 2, 2, i, z0 + 2, 2)
                    elif after:
                        after()

                with act.Fori(0, KD - 1) as i:
                    step(i, False)
                step(KD - 1, True)

            gates(B_GC, Z_GC, C_GC, 8, lambda: ring_hi_of(B_A, 0, 0, Z_A, 0), attention=True)

            act.wait_ge(pair3_read, 2 + SG + NT)
            for j in range(KB):
                z, b = Z_A + 3 * j, B_A + 3 * j
                ring_hi_of(b + 1, 0, 0, z + 1, 0)
                act.wait_ge(z_done, z + 1)
                act.wait_ge(dve_z, 15 + 2 * j)
                act.activation(a_c[:, :], pair(z % 2), ACT.Identity, bias=bias_sb[:, C_A + 3 * j:C_A + 3 * j + 1]).then_inc(act_z, 1)
                ring_hi_of(b + 2, 0, 0, z + 2, 0)
                ring_hi_of(b + 3, 0, 0, z + 3, 0)
                act.wait_ge(dve_z, 18 + 2 * j)
                act.activation(y_hi[:, j, :], a_y[:, :], ACT.Copy).then_inc(y_hi_done, 1)
            gates(B_GA, Z_GA, C_GA, 24, lambda: ring_hi_of(B_GB, 0, 0, Z_GB, 0))
            act.wait_ge(z_done, Z_GB)
            for n in range(KB):
                act.activation(y_hi[:, n, :], q[:, n, :], ACT.Copy).then_inc(y_hi_done, 1)

            def out_hi():
                act.wait_ge(y_lo_done, 3 * KB)
                for c in range(4):
                    hi(B_OUT + c, 0, 0, wide_q_hi[:, :, c * P:(c + 1) * P])

            gates(B_GB, Z_GB, C_GB, 32, before=out_hi)
            for k in range(KD):
                act.wait_ge(merge_add, KD + k + 1)
                act.activation(h_hi[:, k, :], merged[:, k, :], ACT.Copy).then_inc(m_hi, 1)
            act.wait_ge(z_done, Z_FF)
            for c in range(4):
                hi(B_OUT + 4 + c, 0, 0, wide_y_hi[:, :, c * P:(c + 1) * P])
            for t in range(NT):
                act.wait_ge(x1_add, NT + t + 1)
                act.wait_ge(squared, 2 * NT + t)
                rows_squared(x1[:, t, :], 2 * NT + t)
                if t in (2, 3):
                    ring_hi_of(B_FF + t - 2, 0, 0, Z_FF + t - 2, 0)
                if t:
                    act.wait_ge(turned, NT + t)
                    act.activation(h_hi[:, :, (t - 1) * P:t * P],
                                   pair(2 + (t - 1) % 2).rearrange("p (k n) -> p k n", n=P), ACT.Copy).then_inc(turned_hi, 1)
            act.wait_ge(turned, 2 * NT)
            act.activation(h_hi[:, :, (NT - 1) * P:], pair(3).rearrange("p (k n) -> p k n", n=P), ACT.Copy).then_inc(turned_hi, 1)
            act.wait_ge(zeroed, 5)

            def up_evac(z, i, dst):
                act.wait_ge(z_done, z + 1 + 4 * i)
                act.activation(dst[:, 2:], pair(z % 2), ACT.Copy).then_inc(act_z, 1)

            def silu(n, i):
                act.wait_ge(conv_done, n + 4 * i)
                act.activation(conv_g[:, :], conv_g[:, :], ACT.Silu).then_inc(silu_done, 1)

            def last_val(i, row=1):
                act.wait_ge(conv_done, 4 * i - 2)
                up_evac(Z_FF - 1, i, up_v)
                act.wait_ge(act_made, 2 * i)
                act.activation(y_hi[:, row, :], conv_v[:, :], ACT.Copy).then_inc(y_hi_done, 1)

            def ffn(i, first=False, last=False):
                if not first:
                    ring_hi_of(B_FF, 6, i, Z_FF, 4)
                    last_val(i)
                    ring_hi_of(B_FF + 1, 6, i, Z_FF + 1, 4)
                    act.wait_ge(conv_done, 4 * i - 1)
                up_evac(Z_FF, i, up_g)
                ring_hi_of(B_FF + 2, 6, i, Z_FF + 2, 4)
                silu(1, i)
                if first:
                    act.wait_ge(o_done, NT)
                elif not last:
                    act.wait_ge(d_done, NT * i)
                for c in range(2):
                    hi(B_FF + 3 + c, 6, i, (wd_last_hi if last else wd_hi)[:, c, :])
                if not first:
                    act.wait_ge(conv_done, 4 * i)
                up_evac(Z_FF + 1, i, up_v)
                ring_hi_of(B_FF + 5, 6, i, Z_FF + 3, 4)
                act.wait_ge(act_made, 2 * i + 1)
                act.activation(y_hi[:, 2 if last else 0, :], conv_v[:, :], ACT.Copy).then_inc(y_hi_done, 1)
                act.wait_ge(conv_done, 4 * i + 1)
                up_evac(Z_FF + 2, i, up_g)
                silu(3, i)

            ffn(0, first=True)
            with act.Fori(1, FF_STEPS - 1) as i:
                ffn(i)
            ffn(FF_STEPS - 1, last=True)
            last_val(FF_STEPS, 3)

        @block.vector
        def _(dve):
            n = Count()

            def lo(const, per, i, dst, part, tiles=KD):
                src = raw_sv[:, const, :] if const < B_K else raw[:, const % 2, 0:tiles * P]
                if len(dst.shape) == 3:
                    src = src.rearrange("p (k n) -> p k n", n=dst.shape[2])
                dve.wait_ge(w_hi, const + 1 + per * i)
                dve.tensor_tensor(dst, src, part.bitcast(F32), ALU.subtract).then_inc(w_lo, 1)

            def ring_lo_of(const, per, i, z, tiles=KD):
                w = tiles * P
                lo(const, per, i, ring_lo[:, z % 2, 0:w], ring_hi[:, z % 2, 0:w], tiles)

            dve.wait_ge(norm_in, 32)
            seen, x_rs, v_rs = 0, {}, {}
            for step in range(-1, NT + 2):
                for kind, t in squared_at(step):
                    seen += 1
                    (x_rs if kind == "x" else v_rs)[t] = seen
            for step in range(NT + 3):
                if step < NT:
                    t = step
                    dve.wait_ge(rs_ready, x_rs[t])
                    dve.scalar_tensor_tensor(out=x_in[:, t % 4, :], in0=x_in[:, t % 4, :], scalar=rs[:, t:t + 1],
                                             in1=mix_g_sb[:, :], op0=ALU.mult, op1=ALU.mult).then_inc(x_norm_ready, 1)
                t = step - 1
                if 0 <= t < NT:
                    dve.wait_ge(turned_hi, t + 1)
                    cols = slice(t * P, (t + 1) * P)
                    dve.tensor_tensor(h_lo[:, :, cols], pair(t % 2).rearrange("p (k n) -> p k n", n=P),
                                      h_hi[:, :, cols].bitcast(F32), ALU.subtract).then_inc(dve_z, 1)
                if step in (0, 1):
                    for b in ((0,), (2, 3))[step]:
                        cols = slice(b * P, (b + 1) * P)
                        lo(b, 0, 0, wide_y_lo[:, :, cols], wide_y_hi[:, :, cols])
                t = step - 2
                if 0 <= t < NT:
                    if t == 0:
                        dve.wait_ge(row_in, 16)
                    dve.wait_ge(sv_done, t + 1)
                    dve.tensor_tensor(vhat[:, t, :], psum[:, 4 + t % 2, :], row_sb[:, :], ALU.add).then_inc(sv_biased, 1)
                t = step - 3
                if 0 <= t < NT:
                    dve.wait_ge(rs_ready, v_rs[t])
                    dve.tensor_scalar(vhat[:, t, :], vhat[:, t, :], rs[:, NT + t:NT + t + 1], None,
                                      ALU.mult).then_inc(vhat_ready, 1)

            def qk_means(m):
                dve.wait_ge(qk_sum, m + 1)
                src = psum[:, 4 if m in (1, 4) else 6, 0:2 * NT]
                dve.tensor_scalar(meansq_qk[:, m, :], src, 1.0 / HD, EPS, ALU.mult, ALU.add).then_inc(qk_mean, 1)

            def qk_norm(m):
                dve.wait_ge(qk_turned, m + 1)
                raw_t = raw_k[:, :] if m == 0 else q[:, m - 1, :]
                dst = k_pad[:, CHUNK:] if m == 0 else q[:, m - 1, :]
                gain = k_gain_sb if m == 0 else q_scale_sb
                dve.scalar_tensor_tensor(out=dst, in0=raw_t, scalar=gain[:, 0:1], in1=pair(2),
                                         op0=ALU.mult, op1=ALU.mult).then_inc(pair2_read, 1)

            def windows(half):
                dve.wait_ge(v_turned, half + 1)
                dve.tensor_copy(v_win[:, 8 * half:8 * half + 8, :].rearrange("p a b -> p (a b)"), pair(3)).then_inc(pair3_read, 1)

            dve.wait_ge(c_in, 16 * 10)
            dve.tensor_copy(sink_sb[:, 4:8], sink_sb[:, 0:4]).then_inc(dve_step, 1)
            dve.tensor_scalar(q_scale_sb[:, :], q_gain_sb[:, :], HD ** -0.5, None, ALU.mult).then_inc(dve_step, 1)
            n.up()
            dve.wait_ge(dve_step, n.up())
            dve.wait_ge(w_lo, B_Q)
            ring_lo_of(B_Q, 0, 0, Z_Q)
            qk_means(0)
            ring_lo_of(B_Q + 1, 0, 0, Z_Q + 1)
            qk_norm(0)
            ring_lo_of(B_Q + 2, 0, 0, Z_Q + 2)
            windows(0)
            qk_means(1)
            ring_lo_of(B_Q + 3, 0, 0, Z_Q + 3)
            windows(1)
            qk_means(2)
            ring_lo_of(B_U, 0, 0, Z_U)
            qk_norm(1)
            qk_means(3)
            ring_lo_of(B_U + 1, 0, 0, Z_U + 1)
            qk_norm(2)

            def split_y(row, src, k):
                dve.wait_ge(y_hi_done, k)
                dve.tensor_tensor(y_lo[:, row, :], src, y_hi[:, row, :].bitcast(F32), ALU.subtract).then_inc(y_lo_done, 1)
                dve.wait_ge(y_lo_done, k)

            dve.wait_ge(row_in, 32)
            for g in range(SG):
                if g < 2:
                    ring_lo_of(B_U + g + 2, 0, 0, Z_U + g + 2)
                if g == 0:
                    qk_norm(3)
                if g == 1:
                    qk_means(4)
                if g == 2:
                    qk_norm(4)
                if g == SG - 1:
                    ring_lo_of(B_GC, 0, 0, Z_GC)
                dve.wait_ge(mixed, g + 1)
                dve.scalar_tensor_tensor(
                    out=prod[:, :].rearrange("p (a b) -> p a b", b=P), in0=pair(3).rearrange("p (a b) -> p a b", b=P),
                    scalar=sgu_g_sb[:, g:g + 1], in1=row_sb[:, g * P:(g + 1) * P].unsqueeze(1).to_broadcast([P, NT, P]),
                    op0=ALU.mult, op1=ALU.add).then_inc(pair3_read, 1)
                dve.wait_ge(pair3_read, 3 + g)
                dve.wait_ge(act_z, 7 + g)
                dve.tensor_tensor(prod[:, :], prod[:, :], gate[:, :], ALU.mult).then_inc(y_ready, 1)
                split_y(g, prod[:, :], g + 1)

            def merge(i, z0, act0, into):
                dve.wait_ge(z_done, z0 + 2 + 2 * i)
                dve.wait_ge(act_z, act0 + 1 + i)
                row = merged[:, bass.ds(i, 1), :].rearrange("p a b -> p (a b)")
                if not into:
                    dve.tensor_tensor(row, pair(1), gate[:, :], ALU.mult).then_inc(dve_z, 1)
                    return
                dve.tensor_tensor(prod[:, :], pair(1), gate[:, :], ALU.mult).then_inc(dve_z, 1)
                dve.wait_ge(dve_z, into + i)
                dve.tensor_tensor(row, row, prod[:, :], ALU.add).then_inc(merge_add, 1)
                dve.wait_ge(merge_add, into - 24 + i)

            def softmax_shift(i):
                tiles = probs[:, :].rearrange("p (a b) -> p a b", b=P)
                dve.wait_ge(scores, i + 1)
                dve.tensor_tensor(probs[:, :], pair(2), alibi_sb[:, :, :].rearrange("p a b -> p (a b)"), ALU.add).then_inc(pair2_read, 1)
                dve.wait_ge(pair2_read, 6 + i)
                dve.tensor_reduce(peak[:, :], tiles, AX_X, ALU.max).then_inc(dve_step, 1)
                dve.wait_ge(dve_step, n.up())
                dve.tensor_tensor(peak[:, :], peak[:, :], sink_sb[:, :], ALU.max).then_inc(dve_step, 1)
                dve.wait_ge(dve_step, n.up())
                dve.tensor_tensor(tiles, tiles, peak[:, :].unsqueeze(2).to_broadcast([P, 8, P]), ALU.subtract).then_inc(shifted, 1)
                dve.tensor_tensor(sink_e[:, :], sink_sb[:, :], peak[:, :], ALU.subtract).then_inc(shifted, 1)
                dve.tensor_copy(alibi_sb[:, 0, :], alibi_sb[:, 1, :]).then_inc(dve_step, 1)
                dve.wait_ge(dve_step, n.up())

            def softmax_scale(i):
                tiles = probs[:, :].rearrange("p (a b) -> p a b", b=P)
                dve.wait_ge(exps, 2 * i + 2)
                dve.tensor_reduce(denom[:, :], tiles, AX_X, ALU.add).then_inc(dve_step, 1)
                dve.wait_ge(dve_step, n.up())
                dve.tensor_tensor(denom[:, :], denom[:, :], sink_e[:, :], ALU.add).then_inc(dve_step, 1)
                dve.wait_ge(dve_step, n.up())
                dve.reciprocal(denom[:, :], denom[:, :]).then_inc(dve_step, 1)
                dve.wait_ge(dve_step, n.up())
                dve.tensor_tensor(tiles, tiles, denom[:, :].unsqueeze(2).to_broadcast([P, 8, P]), ALU.mult).then_inc(probs_ready, 1)

            def attention_out(i):
                dve.wait_ge(attended, i + 1)
                for g in range(2):
                    rows = slice(g * HD, (g + 1) * HD)
                    for c in range(2):
                        o = dve.tensor_copy(q[rows, :, bass.ds(i * P + c * CHUNK, CHUNK)],
                                            psum[rows, 6 + c, g * 256:(g + 1) * 256].rearrange("p (j t) -> p j t", t=CHUNK))
                        o.then_inc(pair3_read if g + c == 2 else dve_step, 1)
                for _ in range(3):
                    n.up()

            def gates(b0, z0, act0, into, after, attention=False):
                def step(i, last):
                    if attention:
                        softmax_shift(i)
                    ring_lo_of(b0 + 1, 2, i, z0 + 1, KB)
                    if attention:
                        softmax_scale(i)
                    if last:
                        after()
                    else:
                        ring_lo_of(b0 + 2, 2, i, z0 + 2)
                    merge(i, z0, act0, into)
                    if attention:
                        attention_out(i)
                per = 9 if attention else 0
                with dve.Fori(0, KD - 1) as i:
                    n.enter(i, 0, per)
                    step(i, False)
                n.leave(KD - 1)
                step(KD - 1, True)

            dve.wait_ge(alibi_in, 16)
            gates(B_GC, Z_GC, 10, 0, lambda: ring_lo_of(B_A, 0, 0, Z_A), attention=True)
            dve.wait_ge(zeroed, 3)

            def taps(dst, src, w, done, between=None):
                dve.tensor_scalar(dst, src[:, 2:], w(2), None, ALU.mult).then_inc(dve_step, 1)
                dve.wait_ge(dve_step, n.up())
                dve.scalar_tensor_tensor(out=dst, in0=src[:, 1:1 + S], scalar=w(1), in1=dst,
                                         op0=ALU.mult, op1=ALU.add).then_inc(dve_step, 1)
                if between:
                    between()
                dve.wait_ge(dve_step, n.up())
                dve.scalar_tensor_tensor(out=dst, in0=src[:, 0:S], scalar=w(0), in1=dst,
                                         op0=ALU.mult, op1=ALU.add).then_inc(done, 1)

            for j in range(KB):
                z, b, col = Z_A + 3 * j, B_A + 3 * j, C_A + 3 * j
                ring_lo_of(b + 1, 0, 0, z + 1)
                ring_lo_of(b + 2, 0, 0, z + 2)
                dve.wait_ge(act_z, 19 + j)
                dve.wait_ge(z_done, z + 2)
                dve.scalar_tensor_tensor(out=a_ch[:, 2:], in0=pair((z + 1) % 2), scalar=bias_sb[:, col + 1:col + 2],
                                         in1=a_c[:, :], op0=ALU.add, op1=ALU.mult).then_inc(dve_z, 1)
                dve.wait_ge(dve_z, 17 + 2 * j)
                taps(a_conv[:, :], a_ch, lambda tap: conv_a_sb[:, 3 * j + tap:3 * j + tap + 1], dve_step)
                dve.wait_ge(dve_step, n.up())
                ring_lo_of(b + 3, 0, 0, z + 3)
                dve.wait_ge(z_done, z + 3)
                dve.scalar_tensor_tensor(out=a_y[:, :], in0=pair(z % 2), scalar=bias_sb[:, col + 2:col + 3],
                                         in1=a_conv[:, :], op0=ALU.add, op1=ALU.mult).then_inc(dve_z, 1)
                dve.wait_ge(dve_z, 18 + 2 * j)
                split_y(j, a_y[:, :], KB + 1 + j)

            gates(B_GA, Z_GA, 22, 25, lambda: ring_lo_of(B_GB, 0, 0, Z_GB))
            for r in range(KB):
                split_y(r, q[:, r, :], 2 * KB + 1 + r)
            dve.wait_ge(merge_add, KD)

            def out_lo(first, wide_hi, wide_lo):
                for c in range(4):
                    cols = slice(c * P, (c + 1) * P)
                    lo(first + c, 0, 0, wide_lo[:, :, cols], wide_hi[:, :, cols])

            def merged_lo(first, last):
                for k in range(first, last):
                    dve.wait_ge(m_hi, k + 1)
                    dve.tensor_tensor(h_lo[:, k, :], merged[:, k, :], h_hi[:, k, :].bitcast(F32), ALU.subtract).then_inc(m_lo, 1)

            def before_last():
                out_lo(B_OUT, wide_q_hi, wide_q_lo)
                merged_lo(0, 4)

            gates(B_GB, Z_GB, 30, 33, before_last)
            merged_lo(4, KD)
            out_lo(B_OUT + 4, wide_y_hi, wide_y_lo)
            for half in range(2):
                for t in range(NT):
                    if half == 0 and t % 2 == 0:
                        dve.wait_ge(xt_in[t // 2], 48)
                    dve.wait_ge(o_done, half * NT + t + 1)
                    bank = FIRST_BANKS[t] if half == 0 else t % 4
                    dst = x1[:, t, half * HALF:(half + 1) * HALF]
                    dve.tensor_tensor(dst, dst, psum[:, bank, :], ALU.add).then_inc(x1_add, 1)
                    if half == 0:
                        continue
                    if t == 0:
                        dve.wait_ge(ffn_g_in, 16)
                    if t >= 2:
                        dve.wait_ge(turned, NT + t - 1)
                    dve.wait_ge(rs_ready, 2 * NT + t + 1)
                    dve.scalar_tensor_tensor(out=x_norm[:, t % 2, :], in0=x1[:, t, :], scalar=rs[:, 2 * NT + t:2 * NT + t + 1],
                                             in1=ffn_g_sb[:, :], op0=ALU.mult, op1=ALU.mult).then_inc(x_norm_ready, 1)
                    if t in (2, 3):
                        ring_lo_of(B_FF + t - 2, 0, 0, Z_FF + t - 2)
                    for r in ([t - 1] if t else []) + ([t] if t == NT - 1 else []):
                        dve.wait_ge(turned_hi, NT + r + 1)
                        cols = slice(r * P, (r + 1) * P)
                        dve.tensor_tensor(h_lo[:, :, cols], pair(2 + r % 2).rearrange("p (k n) -> p k n", n=P),
                                          h_hi[:, :, cols].bitcast(F32), ALU.subtract).then_inc(turned_lo, 1)

            def up_taps(dst, src, c, i, between=None):
                taps(dst[:, :], src, lambda tap: conv_f_sb[:, bass.ds(3 * c + tap + 12 * i, 1)], conv_done, between)

            def inner(r, i, row, between=None):
                dve.wait_ge(silu_done, 2 * i + r + 1)
                dve.tensor_tensor(conv_v[:, :], conv_v[:, :], conv_g[:, :], ALU.mult).then_inc(act_made, 1)
                if between:
                    between()
                dve.wait_ge(act_made, 2 * i + r + 1)
                dve.wait_ge(y_hi_done, 3 * KB + 2 * i + r + 1)
                dve.tensor_tensor(y_lo[:, row, :], conv_v[:, :], y_hi[:, row, :].bitcast(F32), ALU.subtract).then_inc(y_lo_done, 1)
                dve.wait_ge(y_lo_done, 3 * KB + 2 * i + r + 1)

            def add_down(i, tiles=range(NT)):
                for t in tiles:
                    dve.wait_ge(d_done, NT * i + t - NT + 1)
                    dve.tensor_tensor(x1[:, t, :], x1[:, t, :], pair(2 + t % 2), ALU.add).then_inc(x1_add, 1)

            def last_val(i, row=1, added=None):
                first, second = [(lambda t=t: add_down(added, (t,))) if added else None for t in range(2)]
                dve.wait_ge(act_z, 38 + 4 * i)
                up_taps(conv_v, up_v, -1, i, first)
                dve.wait_ge(conv_done, 4 * i)
                inner(1, i - 1, row, second)

            def ffn(i, first=False, last=False):
                if not first:
                    ring_lo_of(B_FF, 6, i, Z_FF)
                    last_val(i)
                    ring_lo_of(B_FF + 1, 6, i, Z_FF + 1)
                add = not (first or last)
                dve.wait_ge(act_z, 39 + 4 * i)
                up_taps(conv_g, up_g, 0, i, (lambda: add_down(i, (0,))) if add else None)
                if add:
                    add_down(i, (1, 2))
                ring_lo_of(B_FF + 2, 6, i, Z_FF + 2)
                if add:
                    add_down(i, range(3, NT))
                w_of = (wd_last_hi, wd_last_lo) if last else (wd_hi, wd_lo)
                for c in range(2):
                    lo(B_FF + 3 + c, 6, i, w_of[1][:, c, :], w_of[0][:, c, :])
                ring_lo_of(B_FF + 5, 6, i, Z_FF + 3)
                dve.wait_ge(act_z, 40 + 4 * i)
                up_taps(conv_v, up_v, 1, i)
                dve.wait_ge(conv_done, 4 * i + 2)
                inner(0, i, 2 if last else 0)
                dve.wait_ge(act_z, 41 + 4 * i)
                up_taps(conv_g, up_g, 2, i)

            ffn(0, first=True)
            with dve.Fori(1, FF_STEPS - 1) as i:
                n.enter(i, 1, 8)
                ffn(i)
            n.leave(FF_STEPS - 2)
            ffn(FF_STEPS - 1, last=True)
            last_val(FF_STEPS, 3, FF_STEPS - 1)
            add_down(FF_STEPS - 1, range(2, NT))
            add_down(FF_STEPS)

        @block.tensor
        def _(pe):
            def product(z, r_hi, r_lo, tiles, halves=(0, 1)):
                s = z % 2
                for k in range(tiles):
                    w = slice(k * P, (k + 1) * P)
                    for part, (weights, moving) in enumerate(((ring_hi, r_hi), (ring_hi, r_lo), (ring_lo, r_hi))):
                        for half in halves:
                            mm = pe.matmul(psum[:, 2 * s + half, :], weights[:, s, w],
                                           moving[:, k, half * HALF:(half + 1) * HALF],
                                           start=(k == 0 and part == 0), stop=(k == tiles - 1 and part == 2))
                return mm

            def rows_product(bank, t, a_hi, a_lo, wide_hi, wide_lo, ks=range(KD)):
                rows = slice(t * P, (t + 1) * P)
                for k in ks:
                    for part, (a, w) in enumerate(((a_hi, wide_hi), (a_hi, wide_lo), (a_lo, wide_hi))):
                        mm = pe.matmul(psum[:, bank, :], a[:, k, rows], w[:, k, :],
                                       start=(k == 0 and part == 0), stop=(k == KD - 1 and part == 2))
                return mm

            def turn_rows(dst, src):
                for k in range(KD):
                    mm = pe.transpose(dst[:, k * P:(k + 1) * P], src[:, k * P:(k + 1) * P], ident_sb[:, :])
                mm.then_inc(turned, 1)

            pe.wait_ge(norm_in, 32)
            for step in range(NT + 1):
                if step < NT:
                    pe.wait_ge(x_norm_ready, step + 1)
                    if step >= 2:
                        pe.wait_ge(dve_z, step - 1)
                    turn_rows(pair(step % 2), x_in[:, step % 4, :])
                t = step - 1
                if t >= 0:
                    if t == 0:
                        pe.wait_ge(w_lo, 4)
                    pe.wait_ge(dve_z, t + 1)
                    if t >= 2:
                        pe.wait_ge(sv_biased, t - 1)
                    rows_product(4 + t % 2, t, h_hi, h_lo, wide_y_hi, wide_y_lo).then_inc(sv_done, 1)

            def ring(z, before):
                pe.wait_ge(w_lo, z + 5)
                if before:
                    pe.wait_ge(act_z, before)
                product(z, h_hi, h_lo, KD).then_inc(z_done, 1)

            def head_sums(m):
                pe.wait_ge(qk_sq, m + 1)
                for t in range(NT):
                    mm = pe.matmul(psum[:, 4 if m in (1, 4) else 6, 2 * t:2 * t + 2], square[:, t * P:(t + 1) * P],
                                   ones_sb[:, ::HD], start=True, stop=True)
                mm.then_inc(qk_sum, 1)

            def turn_rs(m):
                pe.wait_ge(qk_rs, m + 1)
                for t in range(NT):
                    mm = pe.transpose(pair(2)[:, t * P:(t + 1) * P],
                                      rs_wide[:, 2 * t:2 * t + 2, :].rearrange("p a b -> p (a b)"), ident_sb[:, :])
                mm.then_inc(qk_turned, 1)

            def turn_v(half):
                pe.wait_ge(act_z, 2)
                pe.wait_ge(zeroed, 2)
                if half:
                    pe.wait_ge(pair3_read, half)
                else:
                    pe.wait_ge(qk_mean, 1)
                for c in range(8):
                    first = (8 * half + c) * CHUNK
                    mm = pe.transpose(pair(3)[:, c * P:(c + 1) * P], v_pad[:, first:first + P], ident_sb[:, :])
                mm.then_inc(v_turned, 1)

            def mix(g):
                if g == 0:
                    pe.wait_ge(vhat_ready, NT)
                    pe.wait_ge(masked, 1)
                    pe.wait_ge(qk_mean, 4)
                else:
                    pe.wait_ge(pair3_read, 2 + g)
                for t in range(NT):
                    mm = pe.matmul(pair(3)[:, t * P:(t + 1) * P], vhat[:, t, g * P:(g + 1) * P], sgu_wt_sb[:, g, :],
                                   start=True, stop=True)
                mm.then_inc(mixed, 1)

            ring(Z_K, 0)
            ring(Z_V, 0)
            pe.wait_ge(sv_biased, NT)
            pe.wait_ge(c_in, 16 * 10)
            head_sums(0)
            ring(Z_Q, 1)
            turn_rs(0)
            turn_v(0)
            ring(Z_Q + 1, 2)
            pe.wait_ge(pair2_read, 1)
            head_sums(1)
            turn_v(1)
            ring(Z_Q + 2, 3)
            pe.wait_ge(pair3_read, 2)
            head_sums(2)
            turn_rs(1)
            ring(Z_Q + 3, 4)
            pe.wait_ge(qk_mean, 3)
            head_sums(3)
            pe.wait_ge(pair2_read, 2)
            turn_rs(2)
            ring(Z_U, 5)
            pe.wait_ge(pair2_read, 3)
            turn_rs(3)
            for g in range(SG):
                if g:
                    ring(Z_U + g, 5 + g)
                if g == 1:
                    pe.wait_ge(pair2_read, 4)
                    head_sums(4)
                if g == 2:
                    turn_rs(4)
                mix(g)

            def score_two(i):
                pe.wait_ge(staged, 2 * i + 2)
                pe.wait_ge(pair2_read, 5 + i)
                for c in range(2):
                    for g in range(2):
                        for j in range(2):
                            o = (2 * g + j) * P
                            mm = pe.matmul(psum[:, 4 + c, o:o + P],
                                           q_st[:, g, c, 2 * j:2 * j + 2, :].rearrange("p j t -> p (j t)"),
                                           k_pad[:, bass.ds(i * P + c * CHUNK, P)], start=True, stop=True)
                mm.then_inc(scores, 1)

            def turn_probs(i):
                pe.wait_ge(probs_ready, i + 1)
                pe.wait_ge(pair3_read, 2 + SG + i)
                for c in range(8):
                    mm = pe.transpose(pair(3)[:, c * P:(c + 1) * P], probs[:, c * P:(c + 1) * P], ident_sb[:, :])
                mm.then_inc(probs_turned, 1)

            def attend(i):
                pe.wait_ge(probs_t_ready, i + 1)
                pe.wait_ge(v_staged, i + 1)
                for c in range(2):
                    for g in range(2):
                        mm = pe.matmul(psum[:, 6 + c, g * 256:(g + 1) * 256], v_st[:, c, :],
                                       probs_t[:, c, g * 256:(g + 1) * 256], start=True, stop=True)
                mm.then_inc(attended, 1)

            def gates(b0, z0, act0, dve0, y0, attention=False):
                with pe.Fori(0, KD) as i:
                    if attention:
                        score_two(i)
                    pe.wait_ge(w_lo, b0 + 1 + 2 * i)
                    pe.wait_ge(act_z, act0 + i)
                    product(z0, h_hi, h_lo, KD).then_inc(z_done, 1)
                    if attention:
                        turn_probs(i)
                    pe.wait_ge(w_lo, b0 + 2 + 2 * i)
                    pe.wait_ge(dve_z, dve0 + i)
                    pe.wait_ge(y_lo_done, y0)
                    product(z0 + 1, y_hi, y_lo, KB).then_inc(z_done, 1)
                    if attention:
                        attend(i)

            gates(B_GC, Z_GC, 10, 8, SG, attention=True)
            with pe.Fori(0, 2) as i:
                for c, waits in enumerate((
                        ((act_z, 18 + 2 * i), (dve_z, 15 + 4 * i)), ((dve_z, 16 + 4 * i),), ((act_z, 19 + 2 * i),),
                        ((dve_z, 17 + 4 * i),), ((dve_z, 18 + 4 * i),), ((act_z, 20 + 2 * i),))):
                    pe.wait_ge(w_lo, B_A + c + 1 + 6 * i)
                    for s, v in waits:
                        pe.wait_ge(s, v)
                    product(Z_A + c, h_hi, h_lo, KD).then_inc(z_done, 1)
            pe.wait_ge(dve_z, 23)
            gates(B_GA, Z_GA, 22, 24, 2 * KB)
            gates(B_GB, Z_GB, 30, 32, 3 * KB)

            pe.wait_ge(act_z, 38)
            pe.wait_ge(pair3_read, 2 + SG + NT)
            pe.wait_ge(w_lo, B_OUT + 4)
            for k in range(KD // 2):
                pe.wait_ge(m_lo, k + 1)
                for t in range(4):
                    rows_product(FIRST_BANKS[t], t, h_hi, h_lo, wide_q_hi, wide_q_lo, (k,))
            pe.wait_ge(m_lo, KD)
            pe.wait_ge(dve_z, 40)
            for t in range(NT):
                rows_product(FIRST_BANKS[t], t, h_hi, h_lo, wide_q_hi, wide_q_lo,
                             range(KD // 2 if t < 4 else 0, KD)).then_inc(o_done, 1)
            pe.wait_ge(w_lo, B_OUT + 8)

            def turn_x1(t):
                pe.wait_ge(x_norm_ready, NT + t + 1)
                if t < 2:
                    pe.wait_ge(x1_add, NT)
                else:
                    pe.wait_ge(turned_lo, t - 1)
                turn_rows(pair(2 + t % 2), x_norm[:, t % 2, :])

            for t in range(NT):
                pe.wait_ge(x1_add, FIRST_BANKS.index(t) + 1 if t < 4 else NT + t - 3)
                rows_product(t % 4, t, h_hi, h_lo, wide_y_hi, wide_y_lo).then_inc(o_done, 1)
                if t:
                    turn_x1(t - 1)

            def up(c, block, i, before):
                pe.wait_ge(w_lo, B_FF + block + 1 + 6 * i)
                pe.wait_ge(act_z, before + 4 * i)
                product(Z_FF + c, h_hi, h_lo, KD).then_inc(z_done, 1)

            def down(i, row=0, w_hi_of=wd_hi, w_lo_of=wd_lo):
                pe.wait_ge(y_lo_done, 3 * KB + 2 * i)
                pe.wait_ge(w_lo, B_FF + 6 * i - 1)
                for t in range(NT):
                    pe.wait_ge(x1_add, NT - 1 + NT * i + t)
                    rows = slice(t * P, (t + 1) * P)
                    for r in range(2):
                        for part, (a, w) in enumerate(((y_hi, w_hi_of), (y_hi, w_lo_of), (y_lo, w_hi_of))):
                            for half in range(2):
                                mm = pe.matmul(psum[:, 4 + 2 * (t % 2) + half, :], a[:, row + r, rows],
                                               w[:, r, half * HALF:(half + 1) * HALF],
                                               start=(r == 0 and part == 0), stop=(r == 1 and part == 2))
                    mm.then_inc(d_done, 1)

            pe.wait_ge(w_lo, B_FF + 2)
            pe.wait_ge(x1_add, NT + 6)
            pe.wait_ge(turned_lo, 4)
            product(Z_FF, h_hi, h_lo, KD, (0,))
            turn_x1(NT - 1)
            pe.wait_ge(x1_add, 2 * NT)
            product(Z_FF + 1, h_hi, h_lo, KD, (0,))
            pe.wait_ge(turned_lo, NT)
            product(Z_FF, h_hi, h_lo, KD, (1,)).then_inc(z_done, 1)
            product(Z_FF + 1, h_hi, h_lo, KD, (1,)).then_inc(z_done, 1)
            up(2, 2, 0, 39)
            up(3, 5, 0, 40)
            with pe.Fori(1, FF_STEPS - 1) as i:
                up(0, 0, i, 37)
                down(i)
                up(1, 1, i, 38)
                up(2, 2, i, 39)
                up(3, 5, i, 40)
            for c, b in enumerate((0, 1, 2, 5)):
                up(c, b, FF_STEPS - 1, 37 + c)
            down(FF_STEPS - 1)
            down(FF_STEPS, 2, wd_last_hi, wd_last_lo)


def blocks(w, cols):
    import numpy as np

    k = w.shape[0] // P
    w = w[:, cols].reshape(k, P, len(cols) // P, P)
    return np.ascontiguousarray(w.transpose(2, 1, 0, 3)).reshape(len(cols) // P, P, k * P)


def kernel(**inputs):
    import concourse.bacc as bacc
    import numpy as np
    from concourse.bass_utils import run_bass_kernel_spmd

    a = {k: np.asarray(v) for k, v in inputs.items()}
    f = np.float32
    ab, ac, ah, qo, ko, vo, uo, so, go = 0, 512, 1024, 1536, 2048, 2176, 2304, 2816, 3328
    tile = np.arange(P)
    half = np.arange(HD)
    cols = [so + np.arange(BR), ko + tile, vo + tile]
    cols += [np.concatenate([qo + j * HD + half, qo + (4 + j) * HD + half]) for j in range(4)]
    cols += [uo + np.arange(BR), go + 2 * D + np.arange(D)]
    for j in range(KB):
        cols += [ac + j * P + tile, ah + j * P + tile, ab + j * P + tile]
    cols += [go + np.arange(D), go + D + np.arange(D)]
    cols = np.concatenate(cols)
    bin_ = a["b_in"][0]
    heads = np.concatenate([np.concatenate([j * HD + half, (4 + j) * HD + half]) for j in range(4)])
    wb = a["w_branch"][0]
    every = np.arange(D)
    ff = np.concatenate([np.concatenate([r * P + tile, FF_TILES * P + r * P + tile]) for r in range(FF_TILES)])
    row, key = np.arange(P), np.arange(P)
    table = np.zeros((P, 2, 2, 2, P), f)
    for g in range(2):
        for j in range(2):
            head = 4 * g + 2 * j + row // CHUNK
            slope = 2.0 ** -(head + 1.0)
            table[:, :, g, j, :] = (-slope[:, None] * np.abs(CHUNK + row % CHUNK - key[:, None]).T)[:, None, :]
    table[:, 0, :, :, 0:CHUNK] = -1e30
    head_ones = (row[:, None] // HD == row[None, :] // HD).astype(f)
    arrays = {
        "x": a["x"][0],
        "w_in": blocks(a["w_in"][0], cols),
        "bias": np.ascontiguousarray(bin_[cols].reshape(-1, P).T),
        "w_branch": np.concatenate([blocks(wb[2], every), blocks(wb[0], every), blocks(wb[1][heads], every)]),
        "w_out": blocks(a["w_out"][0], every),
        "w_up": blocks(a["w_up"][0], ff),
        "w_down": a["w_down"][0].reshape(FF_TILES, P, D),
        "mix_g": a["mix_norm_g"],
        "ffn_g": a["ffn_norm_g"],
        "sv_bias": bin_[None, so:so + BR],
        "sgu_wt": np.ascontiguousarray(a["sgu_w"][0].transpose(2, 0, 1)).reshape(P, SG * P),
        "sgu_b": a["sgu_b"][0].reshape(1, SG * P),
        "sgu_g": np.ascontiguousarray(a["sgu_norm_g"][0].reshape(SG, P).T),
        "conv_a": np.ascontiguousarray(a["conv_a_w"][0].reshape(3, KB, P).transpose(2, 1, 0)).reshape(P, KB * 3),
        "conv_f": np.ascontiguousarray(a["conv_f_w"][0][:, ff].reshape(3, 2 * FF_TILES, P).transpose(2, 1, 0)).reshape(P, -1),
        "q_gain": np.tile(a["q_norm_g"][0], 2)[:, None],
        "k_gain": np.tile(a["k_norm_g"][0], 2)[:, None],
        "sink": np.ascontiguousarray(a["attn_sink"][0].reshape(2, 2, 2).transpose(2, 0, 1)).reshape(2, 4),
        "alibi": table.reshape(P, 2 * HALF),
        "ident": np.eye(P, dtype=f),
        "head_ones": head_ones,
    }
    nc = bacc.Bacc("TRN2", target_bir_lowering=False, num_devices=1)
    arrays = {f"in_{k}": np.ascontiguousarray(v) for k, v in arrays.items()}
    args = [nc.dram_tensor(k, v.shape, mybir.dt.from_np(v.dtype), kind="ExternalInput").ap() for k, v in arrays.items()]
    out = nc.dram_tensor("out", (S, D), F32, kind="ExternalOutput").ap()
    hybrid_layer(nc, *args, out)
    r = run_bass_kernel_spmd(nc, [arrays], core_ids=[0])
    return r.results[0]["out"].reshape(1, S, D)
```
